# Optimizing a Trainium2 kernel written in Bass

```python
import jax, jax.numpy as jnp
from jax import lax
import numpy as np

D_MODEL = 1024
BATCH = 1
SEQ = 1024
DEPTH = 2

CHUNK = 64
N_MIXERS = 2
N_CONV_LAYERS = (DEPTH + N_MIXERS - 1) // N_MIXERS
N_ATTN_LAYERS = DEPTH // N_MIXERS
CONV_WIDTH = 31
N_HEADS = 16
N_KV_HEADS = 4
HEAD_DIM = D_MODEL // N_HEADS
GROUP = N_HEADS // N_KV_HEADS
IDX_HEADS = 8
IDX_DIM = 64
TOPK_MAX = 256
Q_BLOCK = 128
ROPE_THETA = 500000.0
Q_COLS = N_HEADS * HEAD_DIM
KV_COLS = N_KV_HEADS * HEAD_DIM
IQ_COLS = IDX_HEADS * IDX_DIM
ATTN_IN_COLS = Q_COLS + 2 * KV_COLS + IQ_COLS + IDX_DIM + IDX_HEADS
N_GROUPS = 4
EXPERTS_PER_GROUP = 8
N_EXPERTS = N_GROUPS * EXPERTS_PER_GROUP
EXPERT_TOP_K = 2
D_EXPERT = 512
EXPERT_ROWS = 128
NORM_EPS = 1e-6

kernel_name = 'hybrid_conv_dsa_hmoe_stream'

def rms_norm(x, g):
    xf = x.astype(jnp.float32)
    y = xf * lax.rsqrt(jnp.mean(xf * xf, axis=-1, keepdims=True) + NORM_EPS)
    return (y * g.astype(jnp.float32)).astype(x.dtype)

def layer_norm(x, g, b):
    xf = x.astype(jnp.float32)
    mu = jnp.mean(xf, axis=-1, keepdims=True)
    xc = xf - mu
    y = xc * lax.rsqrt(jnp.mean(xc * xc, axis=-1, keepdims=True) + NORM_EPS)
    return (y * g.astype(jnp.float32) + b.astype(jnp.float32)).astype(x.dtype)

def rope_tables(seq, rot):
    inv = ROPE_THETA ** (-jnp.arange(0, rot, 2, dtype=jnp.float32) / rot)
    ang = jnp.arange(seq, dtype=jnp.float32)[:, None] * inv[None, :]
    return jnp.cos(ang), jnp.sin(ang)

def partial_rope(x, cos, sin):
    half = cos.shape[-1]
    rot = 2 * half
    xf = x.astype(jnp.float32)
    x1, x2 = xf[..., :half], xf[..., half:rot]
    c, s = cos[None, :, None, :], sin[None, :, None, :]
    out = jnp.concatenate([x1 * c - x2 * s, x2 * c + x1 * s, xf[..., rot:]], axis=-1)
    return out.astype(x.dtype)

def conformer_conv(h, w_in, b_in, w_dw, b_dw, ln_g, ln_b, w_out, b_out):
    u = h @ w_in + b_in
    a, gate = jnp.split(u, 2, axis=-1)
    u = a * jax.nn.sigmoid(gate)
    u = lax.conv_general_dilated(
        u, w_dw[:, None, :], window_strides=(1,), padding=[(CONV_WIDTH - 1, 0)],
        dimension_numbers=('NWC', 'WIO', 'NWC'), feature_group_count=D_MODEL) + b_dw
    u = jax.nn.silu(layer_norm(u, ln_g, ln_b))
    return u @ w_out + b_out

def dsa_attention(h, w_in, k_ln_g, k_ln_b, w_out):
    B, S, _ = h.shape
    top_k = min(TOPK_MAX, S // 4)
    n_blk = S // Q_BLOCK
    proj = h @ w_in
    splits = np.cumsum([Q_COLS, KV_COLS, KV_COLS, IQ_COLS, IDX_DIM]).tolist()
    q, k, v, qi, ki, wi = jnp.split(proj, splits, axis=-1)
    q = q.reshape(B, S, N_HEADS, HEAD_DIM)
    k = k.reshape(B, S, N_KV_HEADS, HEAD_DIM)
    v = v.reshape(B, S, N_KV_HEADS, HEAD_DIM)
    qi = qi.reshape(B, S, IDX_HEADS, IDX_DIM)
    ki = layer_norm(ki, k_ln_g, k_ln_b)[:, :, None, :]
    cos, sin = rope_tables(S, HEAD_DIM // 4)
    q = partial_rope(q, cos, sin)
    k = partial_rope(k, cos, sin)
    cos_i, sin_i = rope_tables(S, IDX_DIM // 4)
    qi = partial_rope(qi, cos_i, sin_i)
    ki = partial_rope(ki, cos_i, sin_i)[:, :, 0, :]
    wi = wi.astype(jnp.float32) * (IDX_HEADS ** -0.5 * IDX_DIM ** -0.5)
    key_chunk = jnp.arange(S) // CHUNK

    def to_blocks(t):
        return jnp.moveaxis(t.reshape((B, n_blk, Q_BLOCK) + t.shape[2:]), 1, 0)

    q_b = to_blocks(q.reshape(B, S, N_KV_HEADS, GROUP, HEAD_DIM))
    qi_b = to_blocks(qi)
    wi_b = to_blocks(wi)

    def block_fn(args):
        blk, q_t, qi_t, wi_t = args
        q_chunk = (blk * Q_BLOCK + jnp.arange(Q_BLOCK)) // CHUNK
        dots = jnp.einsum('bthd,bsd->bths', qi_t, ki).astype(jnp.float32)
        score = jnp.einsum('bths,bth->bts', jax.nn.relu(dots), wi_t)
        admissible = key_chunk[None, :] <= q_chunk[:, None]
        score = jnp.where(admissible[None], score, -jnp.inf)
        _, idx = lax.top_k(score, top_k)
        k_sel = jax.vmap(lambda kb, ib: kb[ib])(k, idx)
        v_sel = jax.vmap(lambda vb, ib: vb[ib])(v, idx)
        valid = key_chunk[idx] <= q_chunk[None, :, None]
        logits = jnp.einsum('btngd,btknd->btngk', q_t, k_sel).astype(jnp.float32) * (HEAD_DIM ** -0.5)
        logits = jnp.where(valid[:, :, None, None, :], logits, -jnp.inf)
        p = jax.nn.softmax(logits, axis=-1).astype(v.dtype)
        o = jnp.einsum('btngk,btknd->btngd', p, v_sel)
        return o.reshape(B, Q_BLOCK, Q_COLS)

    out = lax.map(block_fn, (jnp.arange(n_blk), q_b, qi_b, wi_b))
    out = jnp.moveaxis(out, 0, 1).reshape(B, S, Q_COLS)
    return out @ w_out

def hierarchical_moe(h, w_group, b_group, w_router, b_router, w_gate, w_up, w_down):
    B, S, D = h.shape
    t = h.reshape(B * S, D)
    n_tok = B * S
    g_logits = (t @ w_group + b_group).astype(jnp.float32)
    g_prob = jax.nn.softmax(g_logits, axis=-1)
    g_idx = jnp.argmax(g_logits, axis=-1)
    g_gate = jnp.take_along_axis(g_prob, g_idx[:, None], axis=-1)
    e_logits = (t @ w_router + b_router).astype(jnp.float32).reshape(n_tok, N_GROUPS, EXPERTS_PER_GROUP)
    e_logits = jnp.take_along_axis(e_logits, g_idx[:, None, None], axis=1)[:, 0]
    top_val, top_idx = lax.top_k(e_logits, EXPERT_TOP_K)
    top_w = jax.nn.softmax(top_val, axis=-1) * g_gate
    n_assign = n_tok * EXPERT_TOP_K
    expert_flat = (g_idx[:, None] * EXPERTS_PER_GROUP + top_idx).reshape(-1).astype(jnp.int32)
    w_flat = top_w.reshape(-1)
    tok_flat = jnp.repeat(jnp.arange(n_tok, dtype=jnp.int32), EXPERT_TOP_K)
    order = jnp.argsort(expert_flat)
    e_sorted = expert_flat[order]
    counts = jnp.bincount(expert_flat, length=N_EXPERTS)
    starts = jnp.cumsum(counts) - counts
    padded = (counts + EXPERT_ROWS - 1) // EXPERT_ROWS * EXPERT_ROWS
    pends = jnp.cumsum(padded)
    pstarts = pends - padded
    dest = pstarts[e_sorted] + jnp.arange(n_assign) - starts[e_sorted]
    n_rows = n_assign + N_EXPERTS * EXPERT_ROWS
    n_blocks = n_rows // EXPERT_ROWS
    buf_tok = jnp.zeros((n_rows,), jnp.int32).at[dest].set(tok_flat[order])
    buf_w = jnp.zeros((n_rows,), jnp.float32).at[dest].set(w_flat[order])
    block_expert = jnp.clip(jnp.searchsorted(pends, jnp.arange(n_blocks) * EXPERT_ROWS, side='right'),
                            0, N_EXPERTS - 1)

    def expert_block(args):
        e, tok, w = args
        xb = t[tok]
        hb = jax.nn.silu(xb @ w_gate[e]) * (xb @ w_up[e])
        return (hb @ w_down[e]) * w[:, None].astype(t.dtype)

    rows = lax.map(expert_block, (block_expert, buf_tok.reshape(n_blocks, EXPERT_ROWS),
                                  buf_w.reshape(n_blocks, EXPERT_ROWS)))
    y = jnp.zeros_like(t).at[buf_tok].add(rows.reshape(n_rows, D))
    return y.reshape(B, S, D)

def setup_inputs(seed: int = 0) -> dict:
    key = jax.random.key(seed)
    ks = jax.random.split(key, 24)
    D = D_MODEL

    def nrm(i, shape, scale):
        return jax.random.normal(ks[i], shape, jnp.float32) * scale

    return {
        'x': nrm(0, (BATCH, SEQ, D), 1.0),
        'mix_norm_g': 1.0 + nrm(1, (DEPTH, D), 0.05),
        'ffn_norm_g': 1.0 + nrm(2, (DEPTH, D), 0.05),
        'final_norm_g': 1.0 + nrm(3, (D,), 0.05),
        'conv_w_in': nrm(4, (N_CONV_LAYERS, D, 2 * D), D ** -0.5),
        'conv_b_in': nrm(5, (N_CONV_LAYERS, 2 * D), 0.02),
        'conv_w_dw': nrm(6, (N_CONV_LAYERS, CONV_WIDTH, D), CONV_WIDTH ** -0.5),
        'conv_b_dw': nrm(7, (N_CONV_LAYERS, D), 0.02),
        'conv_ln_g': 1.0 + nrm(8, (N_CONV_LAYERS, D), 0.05),
        'conv_ln_b': nrm(9, (N_CONV_LAYERS, D), 0.02),
        'conv_w_out': nrm(10, (N_CONV_LAYERS, D, D), D ** -0.5),
        'conv_b_out': nrm(11, (N_CONV_LAYERS, D), 0.02),
        'attn_w_in': nrm(12, (N_ATTN_LAYERS, D, ATTN_IN_COLS), D ** -0.5),
        'idx_k_ln_g': 1.0 + nrm(13, (N_ATTN_LAYERS, IDX_DIM), 0.05),
        'idx_k_ln_b': nrm(14, (N_ATTN_LAYERS, IDX_DIM), 0.02),
        'attn_w_out': nrm(15, (N_ATTN_LAYERS, Q_COLS, D), Q_COLS ** -0.5),
        'moe_w_group': nrm(16, (DEPTH, D, N_GROUPS), D ** -0.5),
        'moe_b_group': nrm(17, (DEPTH, N_GROUPS), 0.01),
        'moe_w_router': nrm(18, (DEPTH, D, N_EXPERTS), D ** -0.5),
        'moe_b_router': nrm(19, (DEPTH, N_EXPERTS), 0.01),
        'moe_w_gate': nrm(20, (DEPTH, N_EXPERTS, D, D_EXPERT), D ** -0.5),
        'moe_w_up': nrm(21, (DEPTH, N_EXPERTS, D, D_EXPERT), D ** -0.5),
        'moe_w_down': nrm(22, (DEPTH, N_EXPERTS, D_EXPERT, D), D_EXPERT ** -0.5),
    }

def reference(x, mix_norm_g, ffn_norm_g, final_norm_g, conv_w_in, conv_b_in, conv_w_dw, conv_b_dw,
              conv_ln_g, conv_ln_b, conv_w_out, conv_b_out, attn_w_in, idx_k_ln_g, idx_k_ln_b,
              attn_w_out, moe_w_group, moe_b_group, moe_w_router, moe_b_router, moe_w_gate,
              moe_w_up, moe_w_down):
    h = x
    for i in range(DEPTH):
        hn = rms_norm(h, mix_norm_g[i])
        j = i // N_MIXERS
        if i % N_MIXERS == 0:
            mix = conformer_conv(hn, conv_w_in[j], conv_b_in[j], conv_w_dw[j], conv_b_dw[j],
                                 conv_ln_g[j], conv_ln_b[j], conv_w_out[j], conv_b_out[j])
        else:
            mix = dsa_attention(hn, attn_w_in[j], idx_k_ln_g[j], idx_k_ln_b[j], attn_w_out[j])
        h = h + mix
        h = h + hierarchical_moe(rms_norm(h, ffn_norm_g[i]), moe_w_group[i], moe_b_group[i],
                                 moe_w_router[i], moe_b_router[i], moe_w_gate[i], moe_w_up[i],
                                 moe_w_down[i])
    return rms_norm(h, final_norm_g)


_drawn_inputs = setup_inputs


def setup_inputs(seed=0):
    import zlib

    import numpy as np

    out = dict(_drawn_inputs(seed))
    spreads = {}
    factors = {'idx_k_ln_b': 3.267, 'moe_b_group': 3.763}
    for name, (base, spread) in spreads.items():
        noise = np.random.default_rng([zlib.crc32(name.encode()), seed]).standard_normal(out[name].shape)
        drawn = base * np.exp(spread * noise) if base else spread * noise
        out[name] = __import__('jax').numpy.asarray(drawn.astype(out[name].dtype))
    for name, factor in factors.items():
        out[name] = (out[name] * factor).astype(out[name].dtype)
    return out
```

```python
from contextlib import ExitStack

import concourse.bass as bass
from concourse import mybir

F32 = mybir.dt.float32
BF16 = mybir.dt.bfloat16
I32 = mybir.dt.int32
U32 = mybir.dt.uint32
ALU = mybir.AluOpType
ACT = mybir.ActivationFunctionType
AX = mybir.AxisListType

P = 128
S = 1024
D = 1024
T = S // P
KT = D // P
HALF = 512
EPS = 1e-6
CW = 31
H, NKV, HD = 16, 4, 64
IH = 8
QC, KVC = H * HD, NKV * HD
ROT = HD // 4
CHUNK = 64
TOPK = 256
ROPE_THETA = 500000.0
INADMISSIBLE, TAKEN = -1e38, -3e38
NG, NPG = 4, 8
NE = NG * NPG
DE = 512
ET = DE // P
NR = NG + NE
TOPE = 2
NOVER = (S * TOPE) // (P + 1)
NBLK = NE + NOVER
NEG = 1e30
WG, WU, WD = 0, KT * DE, 2 * KT * DE
SLOT = 2 * KT * DE + ET * D

V_MIX, V_FFN, V_BIN, V_BDW, V_LNG, V_LNB, V_ROWS = 0, 16, 32, 48, 56, 64, 72


class Shared:

    def semaphore(self, nc, name):
        self.of_block.append(nc.alloc_semaphore(name=name))
        return self.of_block[-1]

    def end_block(self, nc):
        nc.clear_and_free_semaphores(self.of_block)
        self.of_block = []
        nc.all_engine_barrier()


def expert_weights(ring, slot):
    w = ring[:, slot * SLOT:(slot + 1) * SLOT]
    return (w[:, WG:WU].rearrange("p (k n) -> p k n", k=KT),
            w[:, WU:WD].rearrange("p (k n) -> p k n", k=KT),
            w[:, WD:SLOT].rearrange("p (k n) -> p k n", k=ET))


def prefetch_experts(sp, g, layer, slots):
    for u in slots:
        wg, wu, wd = expert_weights(g.ring, u)
        sp.dma_start(wg, g.dram["moe_w_gate"][layer, u].rearrange("(k p) n -> p k n", p=P)).then_inc(g.gu_loaded[layer][u], 16)
        sp.dma_start(wu, g.dram["moe_w_up"][layer, u].rearrange("(k p) n -> p k n", p=P)).then_inc(g.gu_loaded[layer][u], 16)
        sp.dma_start(wd, g.dram["moe_w_down"][layer, u].rearrange("(k p) n -> p k n", p=P)).then_inc(g.down_loaded[layer][u], 16)


def conv_block(nc, g):
    with ExitStack() as ctx:
        def sb(name, shape, dt=F32):
            return ctx.enter_context(nc.sbuf_tensor("c_" + name, shape, dt))

        def sem(name):
            return g.semaphore(nc, "c_" + name)

        h, ring, ps, ident, vecs = g.h, g.ring, g.ps, g.ident, g.vecs
        PAD = CW - 1
        w_in = ring[:, 0:2 * KT * D].rearrange("p (f s k n) -> p f s k n", f=KT, s=2, k=KT)
        w_out = ring[:, 2 * KT * D:3 * KT * D].rearrange("p (k n) -> p k n", k=KT)

        hnT = sb("hnT", [P, KT, S])
        cT = sb("cT", [P, KT, S])
        upad = sb("upad", [P, 2, PAD + S])
        scratch = sb("scratch", [P, 2, HALF])
        vrows = sb("vrows", [V_ROWS, P])
        taps = sb("taps", [P, KT, 32])
        ssum = sb("ssum", [P, T]); rms = sb("rms", [P, T]); rinv = sb("rinv", [P, T])
        wrows = upad[0:CW, 0, 0:D]
        hr = cT[:, 0:2, :]
        rstd = upad[:, 0, 0:S]
        bout = upad[:, 1, 0:D]

        x_loaded = [sem(f"x_loaded{i}") for i in range(T)]
        win_loaded = [sem(f"win_loaded{f}") for f in range(KT)]
        wout_loaded = sem("wout_loaded"); vec_loaded = sem("vec_loaded"); fill = sem("fill")
        made = sem("made"); vec_turned = sem("vec_turned"); vec_ready = sem("vec_ready")
        squared = sem("squared"); meaned = sem("meaned"); rooted = sem("rooted"); step = sem("step")
        hr_ready = sem("hr_ready"); turned = sem("turned"); hnT_ready = sem("hnT_ready")
        gated = sem("gated"); unit_done = sem("unit_done"); u_ready = sem("u_ready"); conv_done = sem("conv_done")
        padded = sem("padded"); summed = sem("summed"); centred = sem("centred"); sq_ready = sem("sq_ready")
        var_done = sem("var_done"); var_eps = sem("var_eps"); dev = sem("dev"); scaled = sem("scaled")
        activated = sem("activated"); out_done = sem("out_done"); h_ready = sem("h_ready"); bout_loaded = sem("bout_loaded")

        NU = 2 * KT

        def banks(n):
            return 2 * (n % 3), 2 * (n % 3) + 1

        MEAN, VAR, OUT = (6, 7), (0, 1), ((2, 3), (4, 5))

        block = ctx.enter_context(nc.Block())

        @block.sync
        def _(sp):
            for i in range(T):
                sp.dma_start(h[:, i, :], g.dram["x"][0, i * P:(i + 1) * P, :]).then_inc(x_loaded[i], 16)
            for f in range(KT):
                for s in range(2):
                    sp.dma_start(w_in[:, f, s, :, :],
                                 g.dram["conv_w_in"][0].rearrange("(k p) n -> p k n", p=P)[:, :, s * D + f * P:s * D + (f + 1) * P]).then_inc(win_loaded[f], 16)
            sp.dma_start(w_out, g.dram["conv_w_out"][0].rearrange("(k p) n -> p k n", p=P)).then_inc(wout_loaded, 16)
            for j in range(NE, NBLK):
                sp.dma_start(g.y_dram[j * P:(j + 1) * P, :], g.dram["x"][0, 0:P, :]).then_inc(fill, 16)
            sp.wait_ge(conv_done, KT)
            sp.dma_start(bout, g.dram["conv_b_out"][0].partition_broadcast(P)).then_inc(bout_loaded, 16)
            prefetch_experts(sp, g, 0, (0,))
            sp.wait_ge(out_done, T)
            prefetch_experts(sp, g, 0, (1,))
            sp.wait_ge(fill, 16 * NOVER)

        @block.gpsimd
        def _(pool):
            pool.memset(ident[:, :], 0.0).then_inc(made, 1)
            pool.memset(g.mean_w[:, :], 1.0 / D).then_inc(made, 1)
            pool.wait_ge(made, 2)
            pool.affine_select(out=ident[:, :], in_=ident[:, :], compare_op=ALU.not_equal, fill=1.0, base=0,
                               pattern=[[-1, P]], channel_multiplier=1).then_inc(made, 1)
            pool.wait_ge(vec_ready, 2)
            pool.memset(upad[:, :, 0:PAD], 0.0).then_inc(padded, 1)

        @block.scalar
        def _(act):
            for row, src in ((V_MIX, g.dram["mix_norm_g"]), (V_FFN, g.dram["ffn_norm_g"]), (V_BIN, g.dram["conv_b_in"]), (V_BDW, g.dram["conv_b_dw"]),
                             (V_LNG, g.dram["conv_ln_g"]), (V_LNB, g.dram["conv_ln_b"])):
                n = src.shape[0] * src.shape[1] // P
                act.dma_start(vrows[row:row + n, :], src.rearrange("l (r c) -> (l r) c", c=P)).then_inc(vec_loaded, 16)
            act.dma_start(wrows, g.dram["conv_w_dw"][0]).then_inc(vec_loaded, 16)
            sq = scratch[:, :, :].rearrange("p a b -> p (a b)")

            def square(i):
                act.wait_ge(x_loaded[i], 16)
                if i >= 1:
                    act.wait_ge(squared, i)
                act.activation(sq, h[:, i, :], ACT.Square, accum_out=ssum[:, i:i + 1]).then_inc(squared, 1)

            square(0)
            for i in range(T):
                if i + 1 < T:
                    square(i + 1)
                act.wait_ge(meaned, i + 1)
                act.activation(rms[:, i:i + 1], ssum[:, i:i + 1], ACT.Sqrt).then_inc(rooted, 1)
            for n in range(NU):
                act.wait_ge(unit_done, n + 1)
                if n >= 2:
                    act.wait_ge(u_ready, n - 1)
                act.activation(scratch[:, n % 2, :], ps[:, banks(n)[1], :], ACT.Sigmoid,
                               bias=vecs[:, V_BIN + KT + n // 2:V_BIN + KT + n // 2 + 1]).then_inc(gated, 1)
            for n in range(NU):
                f, half = n % KT, n // KT
                act.wait_ge(centred, n + 1)
                act.activation(hnT[:, f, half * HALF:(half + 1) * HALF], cT[:, f, half * HALF:(half + 1) * HALF],
                               ACT.Square).then_inc(sq_ready, 1)
            for half in range(2):
                cols = slice(half * HALF, (half + 1) * HALF)
                act.wait_ge(var_eps, half + 1)
                act.activation(rstd[:, cols], rstd[:, cols], ACT.Sqrt).then_inc(dev, 1)
                for f in range(KT):
                    act.wait_ge(scaled, half * KT + f + 1)
                    act.activation(cT[:, f, cols], cT[:, f, cols], ACT.Silu, scale=vecs[:, V_LNG + f:V_LNG + f + 1],
                                   bias=vecs[:, V_LNB + f:V_LNB + f + 1]).then_inc(activated, 1)

        @block.tensor
        def _(pe):
            pe.wait_ge(made, 3)
            pe.wait_ge(vec_loaded, 16 * 7)
            pe.transpose(ps[:, 6, 0:V_ROWS], vrows[:, :], ident[0:V_ROWS, 0:V_ROWS]).then_inc(vec_turned, 1)
            for f in range(KT):
                last = pe.transpose(ps[:, 7, 32 * f:32 * f + CW], wrows[:, f * P:(f + 1) * P], ident[0:CW, 0:CW])
            last.then_inc(vec_turned, 1)
            for i in range(T):
                pe.wait_ge(hr_ready, i + 1)
                if i >= 2:
                    pe.wait_ge(hnT_ready, i - 1)
                tps = ps[:, 2 * (i % 2):2 * (i % 2) + 2, :].rearrange("p b (k c) -> p (b k) c", c=P)
                for k in range(KT):
                    last = pe.transpose(tps[:, k, :], hr[:, i % 2, k * P:(k + 1) * P], ident[:, :])
                last.then_inc(turned, 1)

            def mean_of(f):
                pe.wait_ge(conv_done, f + 1)
                for half in range(2):
                    last = pe.matmul(ps[:, MEAN[half], :], g.mean_w[:, :], cT[:, f, half * HALF:(half + 1) * HALF],
                                     start=(f == 0), stop=(f == KT - 1))
                last.then_inc(summed, 1)

            pe.wait_ge(vec_ready, 2)
            for n in range(NU):
                f, half = n // 2, n % 2
                if half == 0:
                    pe.wait_ge(win_loaded[f], 32)
                if n < 2:
                    pe.wait_ge(hnT_ready, 4 * (half + 1))
                    pe.wait_ge(hnT_ready, 4 + 2 * n + 2 if n < 2 else T)
                if n == 2:
                    pe.wait_ge(hnT_ready, T)
                if n >= 3:
                    pe.wait_ge(u_ready, n - 2)
                for s in range(2):
                    for k in range(KT):
                        last = pe.matmul(ps[:, banks(n)[s], :], w_in[:, f, s, k, :], hnT[:, k, half * HALF:(half + 1) * HALF],
                                         start=(k == 0), stop=(k == KT - 1))
                last.then_inc(unit_done, 1)
                if half == 1 and f >= 2:
                    mean_of(f - 2)
            mean_of(KT - 2)
            mean_of(KT - 1)
            for n in range(NU):
                f, half = n % KT, n // KT
                pe.wait_ge(sq_ready, n + 1)
                last = pe.matmul(ps[:, VAR[half], :], g.mean_w[:, :], hnT[:, f, half * HALF:(half + 1) * HALF],
                                 start=(f == 0), stop=(f == KT - 1))
                if f == KT - 1:
                    last.then_inc(var_done, 1)
            pe.wait_ge(wout_loaded, 16)
            for i in range(T):
                pe.wait_ge(activated, KT * (i // (T // 2) + 1))
                if i >= 2:
                    pe.wait_ge(h_ready, i - 1)
                for b in range(2):
                    for k in range(KT):
                        last = pe.matmul(ps[:, OUT[i % 2][b], :], cT[:, k, i * P:(i + 1) * P], w_out[:, k, b * HALF:(b + 1) * HALF],
                                         start=(k == 0), stop=(k == KT - 1))
                last.then_inc(out_done, 1)

        @block.vector
        def _(dve):
            count = [0]

            def mark(ins):
                count[0] += 1
                ins.then_inc(step, 1)
                return count[0]

            def after(n):
                dve.wait_ge(step, n)

            dve.wait_ge(vec_turned, 2)
            dve.tensor_copy(vecs[:, :], ps[:, 6, 0:V_ROWS]).then_inc(vec_ready, 1)
            dve.tensor_copy(taps[:, :, 0:CW], ps[:, 7, 0:32 * KT].rearrange("p (f j) -> p f j", f=KT)[:, :, 0:CW]).then_inc(vec_ready, 1)
            dve.wait_ge(vec_ready, 2)
            gcol = vecs[:, V_MIX:V_MIX + KT]

            def evacuate(i):
                dve.wait_ge(turned, i + 1)
                tps = ps[:, 2 * (i % 2):2 * (i % 2) + 2, :].rearrange("p b (k c) -> p (b k) c", c=P)
                dve.tensor_tensor(hnT[:, :, i * P:(i + 1) * P], tps, gcol.unsqueeze(2).to_broadcast([P, KT, P]),
                                  ALU.mult).then_inc(hnT_ready, 1)

            for i in range(T):
                dve.wait_ge(squared, i + 1)
                dve.tensor_scalar(ssum[:, i:i + 1], ssum[:, i:i + 1], 1.0 / D, EPS, ALU.mult, ALU.add).then_inc(meaned, 1)
                if i >= 1:
                    evacuate(i - 1)
                dve.wait_ge(rooted, i + 1)
                after(mark(dve.reciprocal(rinv[:, i:i + 1], rms[:, i:i + 1])))
                dve.tensor_scalar(hr[:, i % 2, :], h[:, i, :], rinv[:, i:i + 1], None, ALU.mult).then_inc(hr_ready, 1)
            evacuate(T - 1)

            dve.wait_ge(padded, 1)
            for f in range(KT):
                for half in range(2):
                    n = 2 * f + half
                    dve.wait_ge(gated, n + 1)
                    dve.scalar_tensor_tensor(upad[:, f % 2, PAD + half * HALF:PAD + (half + 1) * HALF], ps[:, banks(n)[0], :],
                                             vecs[:, V_BIN + f:V_BIN + f + 1], scratch[:, n % 2, :], ALU.add, ALU.mult).then_inc(u_ready, 1)
                dve.wait_ge(u_ready, 2 * f + 2)
                before = [0, 0]
                for j in range(CW):
                    for half in range(2):
                        cols = slice(half * HALF, (half + 1) * HALF)
                        src = upad[:, f % 2, j + half * HALF:j + (half + 1) * HALF]
                        if j == 0:
                            before[half] = mark(dve.tensor_scalar(cT[:, f, cols], src, taps[:, f, 0:1], vecs[:, V_BDW + f:V_BDW + f + 1],
                                                                  ALU.mult, ALU.add))
                            continue
                        after(before[half])
                        ins = dve.scalar_tensor_tensor(cT[:, f, cols], src, taps[:, f, j:j + 1], cT[:, f, cols], ALU.mult, ALU.add)
                        if j == CW - 1 and half == 1:
                            after(before[0])
                            ins.then_inc(conv_done, 1)
                        else:
                            before[half] = mark(ins)

            dve.wait_ge(summed, KT)
            for n in range(NU):
                f, half = n % KT, n // KT
                cols = slice(half * HALF, (half + 1) * HALF)
                dve.scalar_tensor_tensor(cT[:, f, cols], ps[:, MEAN[half], :], -1.0, cT[:, f, cols], ALU.mult, ALU.add).then_inc(centred, 1)
            for half in range(2):
                cols = slice(half * HALF, (half + 1) * HALF)
                dve.wait_ge(var_done, half + 1)
                dve.tensor_scalar(rstd[:, cols], ps[:, VAR[half], :], EPS, None, ALU.add).then_inc(var_eps, 1)
                dve.wait_ge(dev, half + 1)
                after(mark(dve.reciprocal(rstd[:, cols], rstd[:, cols])))
                for f in range(KT):
                    dve.tensor_tensor(cT[:, f, cols], cT[:, f, cols], rstd[:, cols], ALU.mult).then_inc(scaled, 1)

            dve.wait_ge(bout_loaded, 16)
            for i in range(T):
                after(mark(dve.tensor_tensor(h[:, i, :], h[:, i, :], bout, ALU.add)))
                dve.wait_ge(out_done, i + 1)
                dve.tensor_tensor(h[:, i, :], ps[:, OUT[i % 2][0]:OUT[i % 2][0] + 2, :].rearrange("p b n -> p (b n)"),
                                  h[:, i, :], ALU.add).then_inc(h_ready, 1)

def attention_block(nc, g):
    with ExitStack() as ctx:
        def sb(name, shape, dt=F32):
            return ctx.enter_context(nc.sbuf_tensor("a_" + name, shape, dt))

        def sem(name):
            return g.semaphore(nc, "a_" + name)

        h, ring, ps, ident, vecs = g.h, g.ring, g.ps, g.ident, g.vecs
        gcol = vecs[:, V_MIX + KT:V_MIX + 2 * KT]
        h_dram = nc.dram_tensor("h_dram", [S, D], F32, kind="Internal").ap()
        CH = KT * HALF

        hnT = ring[:, 0:KT * S].rearrange("p (k s) -> p k s", k=KT)
        w_qi, w_q0, w_q1, w_kv = (ring[:, KT * S + n * CH:KT * S + (n + 1) * CH].rearrange("p (k n) -> p k n", k=KT) for n in range(4))
        tok = ring[:, KT * S:KT * S + CH]
        qtok = [tok[:, n * S:(n + 1) * S] for n in range(2)]
        ktok = [tok[:, 2 * S + n * 2 * KVC:2 * S + (n + 1) * 2 * KVC] for n in range(2)]
        probs = [ring[:, n * S:(n + 1) * S] for n in range(3)]
        probsT = [ring[:, (3 + n) * S:(4 + n) * S].rearrange("p (j q) -> p j q", j=T) for n in range(2)]
        otok = ring[:, 5 * S:6 * S]
        oT = ring[:, 6 * S:7 * S].rearrange("p (k q) -> p k q", k=KT)
        resid = [ring[:, 7 * S:8 * S], tok[:, 3 * S:4 * S]]
        w_out = ring[:, KT * S + CH:KT * S + 3 * CH].rearrange("p (k n) -> p k n", k=KT)
        QT = h[:, :, :].rearrange("p t (c q) -> p t c q", c=KT)

        KTd = sb("KTd", [P, NKV, S])
        V = sb("V", [P, T, KVC])
        qiT = sb("qiT", [P, IH // 2, S])
        kiTd = sb("kiTd", [P, S])
        w_ki = sb("w_ki", [P, KT, HD + IH])
        rope = sb("rope", [P, 2, T, ROT // 2])
        kln = sb("kln", [P, 2, HD])
        kiwi = sb("kiwi", [P, T, HD + IH])
        tmp = sb("tmp", [P, 2, H * ROT])
        tmp2 = sb("tmp2", [P, 2, IH * ROT])
        st = sb("st", [P, 4, T])
        max8 = sb("max8", [P, 8])
        offs = [0]
        for i in range(T):
            offs.append(offs[-1] + P * (i + 1))
        score = sb("score", [P, offs[T] - offs[2]])
        bias = sb("bias", [P, offs[T]], BF16)
        mins = sb("mins", [P, H]); rsum = sb("rsum", [P, 2, H]); rinvs = sb("rinvs", [P, H])
        ssum = sb("ssum", [P, T]); rms = sb("rms", [P, T]); rinv = sb("rinv", [P, T])
        hr = KTd[:, 0:2, :]
        junk = qiT[:, 0, :]
        tokI = [bias[:, n * 1024:(n + 1) * 1024].bitcast(F32) for n in range(2)]
        kin = score[:, 0:T * HD].rearrange("p (t d) -> p t d", t=T)
        kin2 = score[:, T * HD:2 * T * HD].rearrange("p (t d) -> p t d", t=T)

        kidup = score[:, 2 * T * HD:4 * T * HD]

        def sc(i):
            return score[:, offs[i] - offs[2]:offs[i + 1] - offs[2]]

        def bi(i):
            return bias[:, offs[i]:offs[i + 1]]

        squared = sem("squared"); meaned = sem("meaned"); rooted = sem("rooted"); step = sem("step")
        hr_ready = sem("hr_ready"); turned = sem("turned"); hnT_ready = sem("hnT_ready")
        spilled = sem("spilled"); wqi_loaded = sem("wqi_loaded"); wki_loaded = sem("wki_loaded")
        wq_loaded = sem("wq_loaded"); wout_loaded = sem("wout_loaded"); tab_loaded = sem("tab_loaded")
        qi_done = sem("qi_done"); qi_copied = sem("qi_copied"); qi_roped = sem("qi_roped")
        qi_turned = sem("qi_turned"); qiT_ready = sem("qiT_ready")
        ki_var = sem("ki_var"); ki_dev = sem("ki_dev"); ki_ready = sem("ki_ready"); ki_turned = sem("ki_turned")
        kiT_ready = sem("kiT_ready"); dots_done = sem("dots_done"); relu_done = sem("relu_done"); dots_used = sem("dots_used")
        proj_done = sem("proj_done"); q_copied = sem("q_copied"); q_roped = sem("q_roped"); pstep = sem("pstep")
        q_turned = sem("q_turned"); qT_ready = sem("qT_ready")
        qk_done = sem("qk_done"); qk_used = sem("qk_used"); exp_done = sem("exp_done")
        p_turned = sem("p_turned"); pT_a = sem("pT_a"); pT_b = sem("pT_b"); pv_done = sem("pv_done")
        o_ready = sem("o_ready"); resid_loaded = [sem(f"resid_loaded{n}") for n in range(2)]

        dots = [(i, c, hd) for i in range(2, T) for c in range(0, P * (i + 1), HALF) for hd in range(IH)]
        NB = 6
        NS = T * H
        WO_LAG = 3
        qk_order, t_order = [("qk", 0), ("qk", 1)], []
        for s in range(NS + WO_LAG + 1):
            if s + 2 < NS:
                qk_order.append(("qk", s + 2))
            if s < NS:
                t_order.append(("p", s))
            if s >= H and s % H == 1 + (0 if s < NS else 0):
                t_order.append(("o", s // H - 1))
            if s >= H and s % H == WO_LAG:
                qk_order.append(("wo", s // H - 1))
        qk_no = {u: n for n, u in enumerate(qk_order)}
        t_no = {u: n for n, u in enumerate(t_order)}

        def keys(s):
            return P * (s // H + 1)

        def b_count(u):
            return sum(1 for v in t_order[:t_no[u] + 1] if v[0] == "o" or keys(v[1]) > HALF)

        RPT = TOPK // 8
        rounds = [(i, r) for i in range(2, T) for r in range(RPT)]
        EARLY = 112
        LAST = H * (T - 1) - 4

        def rounds_at(s):
            n = len(rounds) - EARLY
            lo, hi = (min(n, -(-n * x // LAST)) for x in (s, s + 1))
            return rounds[EARLY + lo:EARLY + hi]

        def head(s):
            i, hd = s // H, s % H
            return i, hd // 2, slice(HD * (hd % 2), HD * (hd % 2) + HD), hd // (H // NKV)

        block = ctx.enter_context(nc.Block())

        @block.sync
        def _(sp):
            sp.dma_start(h_dram.rearrange("(t p) d -> p t d", p=P), h[:, :, :]).then_inc(spilled, 16)
            w = g.dram["attn_w_in"][0].rearrange("(k p) n -> p k n", p=P)
            sp.dma_start(w_qi, w[:, :, QC + 2 * KVC:QC + 2 * KVC + IH * HD]).then_inc(wqi_loaded, 16)
            sp.dma_start(w_ki[:, :, :], w[:, :, QC + 2 * KVC + IH * HD:]).then_inc(wki_loaded, 16)
            sp.dma_start(w_q0, w[:, :, 0:HALF]).then_inc(wq_loaded, 16)
            sp.dma_start(w_q1, w[:, :, HALF:2 * HALF]).then_inc(wq_loaded, 16)
            sp.dma_start(w_kv, w[:, :, QC:QC + 2 * KVC]).then_inc(wq_loaded, 16)
            sp.wait_ge(proj_done, T)
            sp.dma_start(w_out, g.dram["attn_w_out"][0].rearrange("(k p) n -> p k n", p=P)).then_inc(wout_loaded, 16)
            sp.wait_ge(qT_ready, 3 * T)
            for i in range(T):
                if i >= 2:
                    sp.wait_ge(qk_used, qk_no[("wo", i - 2)] + 1)
                sp.dma_start(resid[i % 2], h_dram[i * P:(i + 1) * P, :]).then_inc(resid_loaded[i % 2], 16)
            sp.wait_ge(qk_used, len(qk_order))
            prefetch_experts(sp, g, 1, (0, 1))

        @block.gpsimd
        def _(pool):
            pool.wait_ge(tab_loaded, 64)
            count = [0]

            def chain(ins):
                count[0] += 1
                ins.then_inc(pstep, 1)
                pool.wait_ge(pstep, count[0])

            def rotate(buf, n, i, done):
                x = buf.rearrange("p (n d) -> p n d", d=HD)[:, :, 0:ROT].rearrange("p n (a c) -> p n a c", a=2)
                half = ROT // 2
                shape = [P, n, half]
                c, s = (rope[:, q, i, :].unsqueeze(1).to_broadcast(shape) for q in range(2))
                t = [tmp[:, q, 0:n * ROT].rearrange("p (n a c) -> p n a c", n=n, a=2) for q in range(2)]
                for a in range(2):
                    pool.tensor_tensor(t[0][:, :, a, :], x[:, :, a, :], c, ALU.mult)
                    last = pool.tensor_tensor(t[1][:, :, a, :], x[:, :, a, :], s, ALU.mult)
                chain(last)
                pool.tensor_tensor(x[:, :, 0, :], t[0][:, :, 0, :], t[1][:, :, 1, :], ALU.subtract)
                last = pool.tensor_tensor(x[:, :, 1, :], t[0][:, :, 1, :], t[1][:, :, 0, :], ALU.add)
                if done is None:
                    chain(last)
                else:
                    last.then_inc(done, 1)

            for i in range(T):
                pool.wait_ge(q_copied, i + 1)
                if i >= 1:
                    pool.wait_ge(q_roped, i)
                rotate(qtok[i % 2], H, i, None)
                rotate(ktok[i % 2], 2 * NKV, i, q_roped)

        @block.scalar
        def _(act):
            for q in range(2):
                act.dma_start(rope[:, q, :, :], g.dram["rope"][q].rearrange("(t p) c -> p t c", p=P)).then_inc(tab_loaded, 16)
            act.dma_start(kln[:, 0, :], g.dram["idx_k_ln_g"][0].partition_broadcast(P)).then_inc(tab_loaded, 16)
            act.dma_start(kln[:, 1, :], g.dram["idx_k_ln_b"][0].partition_broadcast(P)).then_inc(tab_loaded, 16)

            def square(i):
                if i >= 1:
                    act.wait_ge(squared, i)
                act.activation(junk, h[:, i, :], ACT.Square, accum_out=ssum[:, i:i + 1]).then_inc(squared, 1)

            square(0)
            for i in range(T):
                if i + 1 < T:
                    square(i + 1)
                act.wait_ge(meaned, i + 1)
                act.activation(rms[:, i:i + 1], ssum[:, i:i + 1], ACT.Sqrt).then_inc(rooted, 1)

            def copy_qiT(i):
                act.wait_ge(qi_turned, i + 1)
                act.activation(qiT[:, :, i * P:(i + 1) * P], ps[:, 4 + i % 2, :].rearrange("p (c q) -> p c q", q=P), ACT.Copy).then_inc(qiT_ready, 1)

            for i in range(T):
                act.wait_ge(qi_done, i + 1)
                if i >= 2:
                    act.wait_ge(qi_turned, i - 1)
                act.activation(tokI[i % 2], ps[:, i % 2, :], ACT.Copy)
                act.activation(kiwi[:, i, :], ps[:, 2 + i % 2, 0:HD + IH], ACT.Copy).then_inc(qi_copied, 1)
                if i >= 1:
                    copy_qiT(i - 1)
            copy_qiT(T - 1)
            act.wait_ge(ki_var, 1)
            act.activation(st[:, 2, :], st[:, 1, :], ACT.Sqrt).then_inc(ki_dev, 1)
            act.wait_ge(ki_turned, 1)
            act.activation(kiTd[:, :], ps[:, 6:8, :].rearrange("p b n -> p (b n)"), ACT.Copy).then_inc(kiT_ready, 1)
            for n, (i, c, hd) in enumerate(dots):
                w = min(HALF, P * (i + 1) - c)
                act.wait_ge(dots_done, n + 1)
                act.activation(ps[:, n % NB, 0:w], ps[:, n % NB, 0:w], ACT.Relu).then_inc(relu_done, 1)

            act.wait_ge(dots_used, len(dots))
            act.wait_ge(spilled, 16)
            act.wait_ge(hr_ready, T)

            def copy_turned(i):
                for part in range(3):
                    act.wait_ge(q_turned, 3 * i + part + 1)
                    src = ps[:, 6 + part % 2, :].rearrange("p (c q) -> p c q", q=P)
                    dst = QT[:, i, 4 * part:4 * part + 4, :] if part < 2 else KTd[:, :, i * P:(i + 1) * P]
                    act.activation(dst, src, ACT.Copy).then_inc(qT_ready, 1)

            for i in range(T):
                act.wait_ge(proj_done, i + 1)
                if i >= 2:
                    act.wait_ge(q_turned, 3 * (i - 1))
                b = 3 * (i % 2)
                act.activation(qtok[i % 2], ps[:, b:b + 2, :].rearrange("p b n -> p (b n)"), ACT.Copy)
                act.activation(ktok[i % 2].rearrange("p (n a d) -> p n a d", a=2, d=HD),
                               ps[:, b + 2, 0:KVC].rearrange("p (n d) -> p n d", d=HD).unsqueeze(2).to_broadcast([P, NKV, 2, HD]), ACT.Copy)
                act.activation(V[:, i, :], ps[:, b + 2, KVC:2 * KVC], ACT.Copy).then_inc(q_copied, 1)
                if i >= 1:
                    copy_turned(i - 1)
            copy_turned(T - 1)

            def exps(s):
                act.wait_ge(qk_used, qk_no[("qk", s)] + 1)
                buf = probs[s % 3][:, 0:keys(s)]
                act.activation(buf, buf, ACT.Exp, scale=-1.0, bias=mins[:, s % H:s % H + 1],
                               accum_out=rsum[:, (s // H) % 2, s % H:s % H + 1]).then_inc(exp_done, 1)

            def turned_half(u, dst):
                act.wait_ge(p_turned, t_no[u] + 1)
                w = dst.shape[1]
                act.activation(dst, ps[:, 4, 0:w * P].rearrange("p (j q) -> p j q", q=P), ACT.Copy).then_inc(pT_a, 1)

            exps(0)
            exps(1)
            for s in range(NS + WO_LAG + 1):
                if s < NS:
                    if s >= 2:
                        act.wait_ge(pv_done, s - 1)
                    turned_half(("p", s), probsT[s % 2][:, 0:min(4, keys(s) // P), :])
                if ("o", s // H - 1) in t_no and s % H == 1 and s >= H:
                    turned_half(("o", s // H - 1), oT[:, 0:4, :])
                if s + 2 < NS:
                    exps(s + 2)

        @block.tensor
        def _(pe):
            for i in range(T):
                pe.wait_ge(hr_ready, i + 1)
                if i >= 2:
                    pe.wait_ge(hnT_ready, i - 1)
                tps = ps[:, 2 * (i % 2):2 * (i % 2) + 2, :].rearrange("p b (k c) -> p (b k) c", c=P)
                for k in range(KT):
                    last = pe.transpose(tps[:, k, :], hr[:, i % 2, k * P:(k + 1) * P], ident[:, :])
                last.then_inc(turned, 1)

            def turn_qi(i):
                pe.wait_ge(qi_roped, i + 1)
                if i >= 2:
                    pe.wait_ge(qiT_ready, i - 1)
                for c in range(4):
                    last = pe.transpose(ps[:, 4 + i % 2, c * P:(c + 1) * P], tokI[i % 2][:, c * P:(c + 1) * P], ident[:, :])
                last.then_inc(qi_turned, 1)

            def project(bank, w, i, n):
                for k in range(KT):
                    last = pe.matmul(ps[:, bank, 0:n], hnT[:, k, i * P:(i + 1) * P], w[:, k, 0:n], start=(k == 0), stop=(k == KT - 1))
                return last

            pe.wait_ge(hnT_ready, T)
            pe.wait_ge(wqi_loaded, 16)
            pe.wait_ge(wki_loaded, 16)
            for i in range(T):
                if i >= 2:
                    pe.wait_ge(qi_copied, i - 1)
                project(i % 2, w_qi, i, HALF)
                project(2 + i % 2, w_ki, i, HD + IH).then_inc(qi_done, 1)
                if i >= 1:
                    turn_qi(i - 1)
            turn_qi(T - 1)
            pe.wait_ge(ki_ready, 1)
            for i in range(T):
                last = pe.transpose(ps[:, 6 + i // 4, (i % 4) * P:(i % 4 + 1) * P],
                                    kidup[:, i * P:(i + 1) * P], ident[:, :])
            last.then_inc(ki_turned, 1)
            pe.wait_ge(kiT_ready, 1)
            pe.wait_ge(qiT_ready, T)
            for n, (i, c, hd) in enumerate(dots):
                w = min(HALF, P * (i + 1) - c)
                if n >= NB:
                    pe.wait_ge(dots_used, n - NB + 1)
                half = slice(HD * (hd % 2), HD * (hd % 2) + HD)
                pe.matmul(ps[:, n % NB, 0:w], qiT[half, hd // 2, i * P:(i + 1) * P], kiTd[half, c:c + w],
                          start=True, stop=True).then_inc(dots_done, 1)

            def turn_qk(i):
                pe.wait_ge(q_roped, i + 1)
                for part in range(3):
                    if 3 * i + part >= 2:
                        pe.wait_ge(qT_ready, 3 * i + part - 1)
                    if 3 * i + part == 1 or 3 * i + part == 0:
                        pe.wait_ge(kiT_ready, 1)
                    if part == 2 or (part == 0 and i >= 1):
                        pe.wait_ge(qT_ready, 3 * i + part - (0 if part == 0 else 1))
                    for c in range(4):
                        src = (qtok[i % 2][:, (4 * part + c) * P:(4 * part + c + 1) * P] if part < 2 else
                               ktok[i % 2][:, c * P:(c + 1) * P])
                        last = pe.transpose(ps[:, 6 + part % 2, c * P:(c + 1) * P], src, ident[:, :])
                    last.then_inc(q_turned, 1)

            pe.wait_ge(dots_used, len(dots))
            pe.wait_ge(wq_loaded, 48)
            for i in range(T):
                if i >= 2:
                    pe.wait_ge(q_copied, i - 1)
                b = 3 * (i % 2)
                project(b, w_q0, i, HALF)
                project(b + 1, w_q1, i, HALF)
                project(b + 2, w_kv, i, HALF).then_inc(proj_done, 1)
                if i >= 1:
                    turn_qk(i - 1)
            turn_qk(T - 1)
            pe.wait_ge(qT_ready, 3 * T)

            def qk(s):
                i, c, half, n = head(s)
                no = qk_no[("qk", s)]
                if no >= 2:
                    pe.wait_ge(qk_used, no - 1)
                for k0 in range(0, keys(s), HALF):
                    w = min(HALF, keys(s) - k0)
                    last = pe.matmul(ps[:, 2 * (no % 2) + k0 // HALF, 0:w], QT[half, i, c, :], KTd[half, n, k0:k0 + w],
                                     start=True, stop=True)
                last.then_inc(qk_done, 1)

            def turn(u, src, n):
                no = t_no[u]
                if no >= 1:
                    before = t_order[no - 1]
                    pe.wait_ge(pT_a, no)
                    if b_count(before):
                        pe.wait_ge(pT_b, b_count(before))
                for j in range(n):
                    last = pe.transpose(ps[:, 4 + j // 4, (j % 4) * P:(j % 4 + 1) * P], src[:, j * P:(j + 1) * P], ident[:, :])
                last.then_inc(p_turned, 1)

            def pv(s):
                i, _, _, n = head(s)
                pe.wait_ge(pT_a, t_no[("p", s)] + 1)
                if keys(s) > HALF:
                    pe.wait_ge(pT_b, b_count(("p", s)))
                if s % H == 0 and i >= 1:
                    pe.wait_ge(o_ready, i)
                hd = s % H
                for j in range(i + 1):
                    last = pe.matmul(ps[:, 6 + hd // 8, (hd % 8) * HD:(hd % 8 + 1) * HD], probsT[s % 2][:, j, :],
                                     V[:, j, n * HD:(n + 1) * HD], start=(j == 0), stop=(j == i))
                last.then_inc(pv_done, 1)

            def output(i):
                no = qk_no[("wo", i)]
                pe.wait_ge(qk_used, no - 1)
                pe.wait_ge(pT_a, t_no[("o", i)] + 1)
                pe.wait_ge(pT_b, b_count(("o", i)))
                for b in range(2):
                    for k in range(KT):
                        last = pe.matmul(ps[:, 2 * (no % 2) + b, :], oT[:, k, :], w_out[:, k, b * HALF:(b + 1) * HALF],
                                         start=(k == 0), stop=(k == KT - 1))
                last.then_inc(qk_done, 1)

            qk(0)
            qk(1)
            for s in range(NS + WO_LAG + 1):
                if s + 2 < NS:
                    qk(s + 2)
                if s < NS:
                    pe.wait_ge(exp_done, s + 1)
                    turn(("p", s), probs[s % 3], keys(s) // P)
                if 1 <= s <= NS:
                    pv(s - 1)
                if s >= H and s % H == 1:
                    pe.wait_ge(o_ready, s // H)
                    turn(("o", s // H - 1), otok, KT)
                if s >= H and s % H == WO_LAG:
                    if s // H == 1:
                        pe.wait_ge(wout_loaded, 16)
                    output(s // H - 1)

        @block.vector
        def _(dve):
            count = [0]

            def mark(ins):
                count[0] += 1
                ins.then_inc(step, 1)
                return count[0]

            def chain(ins):
                dve.wait_ge(step, mark(ins))

            def evacuate(i):
                dve.wait_ge(turned, i + 1)
                tps = ps[:, 2 * (i % 2):2 * (i % 2) + 2, :].rearrange("p b (k c) -> p (b k) c", c=P)
                dve.tensor_tensor(hnT[:, :, i * P:(i + 1) * P], tps, gcol.unsqueeze(2).to_broadcast([P, KT, P]),
                                  ALU.mult).then_inc(hnT_ready, 1)

            for i in range(T):
                dve.wait_ge(squared, i + 1)
                dve.tensor_scalar(ssum[:, i:i + 1], ssum[:, i:i + 1], 1.0 / D, EPS, ALU.mult, ALU.add).then_inc(meaned, 1)
                if i >= 1:
                    evacuate(i - 1)
                dve.wait_ge(rooted, i + 1)
                chain(dve.reciprocal(rinv[:, i:i + 1], rms[:, i:i + 1]))
                dve.tensor_scalar(hr[:, i % 2, :], h[:, i, :], rinv[:, i:i + 1], None, ALU.mult).then_inc(hr_ready, 1)
            evacuate(T - 1)
            dve.wait_ge(tab_loaded, 64)

            def rotate(x3, cos, sin, n, done):
                x = x3[:, :, 0:ROT].rearrange("p n (a c) -> p n a c", a=2)
                t = [tmp2[:, q, 0:n * ROT].rearrange("p (n a c) -> p n a c", n=n, a=2) for q in range(2)]
                for a in range(2):
                    dve.tensor_tensor(t[0][:, :, a, :], x[:, :, a, :], cos, ALU.mult)
                    last = dve.tensor_tensor(t[1][:, :, a, :], x[:, :, a, :], sin, ALU.mult)
                chain(last)
                dve.tensor_tensor(x[:, :, 0, :], t[0][:, :, 0, :], t[1][:, :, 1, :], ALU.subtract)
                last = dve.tensor_tensor(x[:, :, 1, :], t[0][:, :, 1, :], t[1][:, :, 0, :], ALU.add)
                if done is None:
                    chain(last)
                else:
                    last.then_inc(done, 1)

            for i in range(T):
                dve.wait_ge(qi_copied, i + 1)
                if i >= 1:
                    dve.wait_ge(qi_roped, i)
                cos, sin = (rope[:, q, i, :].unsqueeze(1).to_broadcast([P, IH, ROT // 2]) for q in range(2))
                rotate(tokI[i % 2].rearrange("p (n d) -> p n d", d=HD), cos, sin, IH, qi_roped)
            def bct(v, n):
                return v.unsqueeze(2).to_broadcast([P, T, n])
            ki = kiwi[:, :, 0:HD]
            dve.wait_ge(qi_roped, T)
            chain(dve.tensor_reduce(st[:, 0, :], ki, AX.X, ALU.add))
            chain(dve.tensor_scalar(st[:, 0, :], st[:, 0, :], 1.0 / HD, None, ALU.mult))
            chain(dve.tensor_tensor(kin, ki, bct(st[:, 0, :], HD), ALU.subtract))
            chain(dve.tensor_tensor(kin2, kin, kin, ALU.mult))
            chain(dve.tensor_reduce(st[:, 1, :], kin2, AX.X, ALU.add))
            dve.tensor_scalar(st[:, 1, :], st[:, 1, :], 1.0 / HD, EPS, ALU.mult, ALU.add).then_inc(ki_var, 1)
            dve.wait_ge(ki_dev, 1)
            chain(dve.reciprocal(st[:, 3, :], st[:, 2, :]))
            chain(dve.tensor_tensor(kin, kin, bct(st[:, 3, :], HD), ALU.mult))
            chain(dve.tensor_tensor(kin, kin, kln[:, 0, :].unsqueeze(1).to_broadcast([P, T, HD]), ALU.mult))
            chain(dve.tensor_tensor(kin2, kin, kln[:, 1, :].unsqueeze(1).to_broadcast([P, T, HD]), ALU.add))
            rotate(kin2, rope[:, 0, :, :], rope[:, 1, :, :], T, None)
            dve.tensor_copy(kidup.rearrange("p (t a d) -> p t a d", a=2, d=HD),
                            kin2.unsqueeze(2).to_broadcast([P, T, 2, HD])).then_inc(ki_ready, 1)
            wi = kiwi[:, :, HD:HD + IH]
            chain(dve.tensor_scalar(wi, wi, float(IH) ** -0.5 * float(HD) ** -0.5, None, ALU.mult))

            def edge(ap, i, value):
                n = P * (i + 1)
                return dve.memset(ap[0:CHUNK, n - CHUNK:n], value)

            dve.wait_ge(ki_turned, 1)
            last = {}
            for n, (i, c, hd) in enumerate(dots):
                w = min(HALF, P * (i + 1) - c)
                dst = sc(i)[:, c:c + w]
                dve.wait_ge(relu_done, n + 1)
                if hd == 0:
                    dve.tensor_scalar(dst, ps[:, n % NB, 0:w], kiwi[:, i, HD:HD + 1], None, ALU.mult).then_inc(dots_used, 1)
                else:
                    dve.wait_ge(dots_used, n)
                    dve.scalar_tensor_tensor(dst, ps[:, n % NB, 0:w], kiwi[:, i, HD + hd:HD + hd + 1], dst, ALU.mult, ALU.add).then_inc(dots_used, 1)
            dve.wait_ge(dots_used, len(dots))
            dve.wait_ge(qi_turned, T)
            for i in range(2):
                chain(dve.memset(bi(i), 0.0))
                chain(edge(bi(i), i, -NEG))

            def search(i, r):
                s = sc(i)
                if r == 0:
                    chain(edge(s, i, INADMISSIBLE))
                chain(dve.max(max8[:, :], s))
                chain(dve.match_replace(s, max8[:, :], s, TAKEN))
                if r == RPT - 1:
                    chain(dve.tensor_scalar(bi(i), s, INADMISSIBLE * 2, -NEG, ALU.is_gt, ALU.mult))

            for i, r in rounds[:EARLY]:
                search(i, r)

            def masked(s):
                no = qk_no[("qk", s)]
                dve.wait_ge(qk_done, no + 1)
                if s >= 3:
                    dve.wait_ge(p_turned, t_no[("p", s - 3)] + 1)
                if s >= H:
                    dve.wait_ge(exp_done, s - H + 1)
                n = keys(s)
                b = 2 * (no % 2)
                dve.tensor_tensor_reduce(probs[s % 3][:, 0:n], ps[:, b:b + 2, :].rearrange("p b n -> p (b n)")[:, 0:n], bi(s // H),
                                         -float(HD) ** -0.5, 3e38, ALU.add, ALU.min, mins[:, s % H:s % H + 1]).then_inc(qk_used, 1)

            def turned_half(u, dst):
                dve.wait_ge(p_turned, t_no[u] + 1)
                w = dst.shape[1]
                dve.tensor_copy(dst, ps[:, 5, 0:w * P].rearrange("p (j q) -> p j q", q=P)).then_inc(pT_b, 1)

            def output(i):
                no = qk_no[("wo", i)]
                dve.wait_ge(qk_done, no + 1)
                dve.wait_ge(resid_loaded[i % 2], 16 * (i // 2 + 1))
                b = 2 * (no % 2)
                dve.tensor_tensor(h[:, i, :], ps[:, b:b + 2, :].rearrange("p b n -> p (b n)"), resid[i % 2], ALU.add).then_inc(qk_used, 1)

            dve.wait_ge(qT_ready, 3 * T)
            masked(0)
            masked(1)
            for s in range(NS + WO_LAG + 1):
                if s < NS and keys(s) > HALF:
                    if s >= 2:
                        dve.wait_ge(pv_done, s - 1)
                    turned_half(("p", s), probsT[s % 2][:, 4:keys(s) // P, :])
                if s >= H and s % H == 0:
                    i = s // H - 1
                    dve.wait_ge(pv_done, s)
                    dve.wait_ge(exp_done, s)
                    chain(dve.reciprocal(rinvs[:, :], rsum[:, i % 2, :]))
                    if i >= 1:
                        dve.wait_ge(p_turned, t_no[("o", i - 1)] + 1)
                    dve.tensor_tensor(otok.rearrange("p (n d) -> p n d", d=HD), ps[:, 6:8, :].rearrange("p b (n d) -> p (b n) d", d=HD),
                                      rinvs[:, :].unsqueeze(2).to_broadcast([P, H, HD]), ALU.mult).then_inc(o_ready, 1)
                if s >= H and s % H == 1:
                    turned_half(("o", s // H - 1), oT[:, 4:8, :])
                if s + 2 < NS:
                    masked(s + 2)
                if s >= H and s % H == WO_LAG:
                    output(s // H - 1)
                for i, r in rounds_at(s):
                    search(i, r)

def moe_block(nc, g, layer, after):
    with ExitStack() as ctx:
        pre = f"m{layer}_"

        def sb(name, shape, dt=F32):
            return ctx.enter_context(nc.sbuf_tensor(pre + name, shape, dt))

        def sem(name):
            return g.semaphore(nc, pre + name)

        h, ring, ps, ident = g.h, g.ring, g.ps, g.ident
        gcol = g.vecs[:, V_FFN + 8 * layer:V_FFN + 8 * layer + KT]
        hr_dram = nc.dram_tensor(pre + "hr_dram", [S, D], F32, kind="Internal").ap()
        y_dram = g.y_dram

        sq = sb("sq", [P, D])
        hr = sb("hr", [P, 2, D])
        hnT = sb("hnT", [P, 2, KT, P])
        wr = sb("wr", [P, KT, NR])
        rbias = sb("rbias", [P, NR])
        ssum = sb("ssum", [P, T]); rms = sb("rms", [P, T]); rinv = sb("rinv", [P, T])
        pri = sb("pri", [P, NE])
        iota = sb("iota", [P, P])
        tokid = sb("tokid", [P, T])
        cap1 = sb("cap1", [P, NE])
        zeros = sb("zeros", [P, NE])
        ones_b = sb("ones_b", [P, P], BF16)
        tri_b = sb("tri_b", [P, P], BF16)
        lg = sb("lg", [P, T, NR])
        ga = sb("ga", [P, T, NG]); goh = sb("goh", [P, T, NG])
        em = sb("em", [P, T, NE]); ea = sb("ea", [P, T, NE])
        oh = sb("oh", [P, 2, T, NE]); ohb = sb("ohb", [P, T, NE], BF16)
        small = sb("small", [P, 16, T])
        wts = sb("wts", [P, 2, T])
        novf = sb("novf", [P, NE]); novi = sb("novi", [P, NE], I32); obend = sb("obend", [P, NE])
        dlt = sb("dlt", [P, NE])
        slotm = sb("slotm", [P, T, NE])
        slot = sb("slot", [P, 2, T]); sloti = sb("sloti", [P, 2, T], I32)
        blki = sb("blki", [P, 2, T], I32); loi = sb("loi", [P, 2, T], I32)
        blk = sb("blk", [P, 2, T]); lo = sb("lo", [P, 2, T])
        slotu = sb("slotu", [P, 2 * T], U32)
        Bm = sb("Bm", [P, 2 * T, NBLK])
        toku = sb("toku", [P, NBLK], U32)
        eidc = sb("eidc", [P, NOVER, NE]); eid = sb("eid", [P, NOVER])
        eidi = sb("eidi", [P, NOVER + 1], I32)
        xg = sb("xg", [P, 2, D]); xT = sb("xT", [P, 2, KT, P])
        sg = sb("sg", [P, DE]); hb = sb("hb", [P, DE]); hbT = sb("hbT", [P, ET, P])
        y = sb("y", [P, 2, D])
        Am = hr[:, :, :].rearrange("p a (b c) -> p (a b) c", c=P)

        squared = sem("squared"); meaned = sem("meaned"); rooted = sem("rooted"); step = sem("step")
        hr_ready = sem("hr_ready"); hr_stored = [sem(f"hr_stored{u}") for u in range(2)]
        turned = sem("turned"); hnT_ready = sem("hnT_ready"); routed = sem("routed")
        small_loaded = sem("small_loaded"); consts = sem("consts")
        ebias = sem("ebias"); expd = sem("expd"); ohb_ready = sem("ohb_ready"); ranked = sem("ranked")
        ab_ready = sem("ab_ready"); listed = sem("listed"); lists_ready = sem("lists_ready")
        xg_loaded = [sem(f"xg_loaded{u}") for u in range(2)]
        x_turned = sem("x_turned"); xT_ready = sem("xT_ready")
        gu_done = sem("gu_done"); silu_done = sem("silu_done"); hb_ready = sem("hb_ready")
        h_turned = sem("h_turned"); hbT_ready = sem("hbT_ready"); down_done = sem("down_done")
        y_half0 = sem("y_half0"); y_half1 = sem("y_half1"); y_stored = [sem(f"y_stored{u}") for u in range(2)]
        gu_loaded, down_loaded = g.gu_loaded[layer], g.down_loaded[layer]
        o_loaded = sem("o_loaded"); o_gathered = sem("o_gathered");
        r_loaded = [sem(f"r_loaded{u}") for u in range(2)]; combined = sem("combined")
        f_sq = sem("f_sq"); f_mean = sem("f_mean"); f_root = sem("f_root"); f_out = sem("f_out"); f_stored = [sem(f"f_stored{u}") for u in range(2)]
        if after:
            final_g = sb("final_g", [P, D]); final_loaded = sem("final_loaded")

        TURN = (0, 1)
        GATE, UP, DOWN, HT = 2, 3, (4, 5), 6
        ROUTE, RANK = 7, 6

        def turn_ps():
            return ps[:, 0:2, :].rearrange("p b (k c) -> p (b k) c", c=P)

        def over_loop(eng):
            return eng.value_load(eidi[0:1, NOVER:NOVER + 1], min_val=0, max_val=NOVER)

        block = ctx.enter_context(nc.Block())

        @block.sync
        def _(sp):
            for i in range(T):
                sp.wait_ge(hr_ready, i + 1)
                sp.dma_start(hr_dram[i * P:(i + 1) * P, :], hr[:, i % 2, :]).then_inc(hr_stored[i % 2], 16)

            def load_gu(e, u):
                wg, wu, _ = expert_weights(ring, u)
                sp.dma_start(wg, g.dram["moe_w_gate"][layer, bass.ds(e, 1)].rearrange("e (k p) n -> p (e k) n", p=P)).then_inc(gu_loaded[u], 16)
                sp.dma_start(wu, g.dram["moe_w_up"][layer, bass.ds(e, 1)].rearrange("e (k p) n -> p (e k) n", p=P)).then_inc(gu_loaded[u], 16)

            def load_down(e, u):
                sp.dma_start(expert_weights(ring, u)[2],
                             g.dram["moe_w_down"][layer, bass.ds(e, 1)].rearrange("e (k p) n -> p (e k) n", p=P)).then_inc(down_loaded[u], 16)

            def store_y(e, u):
                sp.wait_ge(y_half0, e + 1)
                sp.wait_ge(y_half1, e + 1)
                sp.dma_start(y_dram[bass.ds(e * P, P), :], y[:, u, :]).then_inc(y_stored[u], 16)

            def after_products(e, u):
                sp.wait_ge(gu_done, e + 1)
                load_gu(e + 2, u)
                sp.wait_ge(down_done, e)
                load_down(e + 1, 1 - u)
                store_y(e - 1, 1 - u)

            sp.wait_ge(gu_done, 1)
            load_gu(2, 0)
            with sp.Fori(0, NE // 2 - 2) as i:
                after_products(2 * i + 1, 1)
                after_products(2 * i + 2, 0)
            after_products(NE - 3, 1)
            sp.wait_ge(down_done, NE - 2)
            load_down(NE - 1, 1)
            for e in range(NE - 3, NE):
                store_y(e, e % 2)
            n_over = over_loop(sp)
            with sp.If(n_over > 0):
                with sp.Fori(0, n_over) as j:
                    e = sp.value_load(eidi[0:1, bass.ds(j, 1)], min_val=0, max_val=NE - 1)
                    wg, wu, wd = expert_weights(ring, 0)
                    sp.wait_ge(down_done, NE + j)
                    sp.wait_ge(y_stored[0], 16 * (NE // 2) + 16 * j)
                    sp.dma_start(wg, g.dram["moe_w_gate"][layer, bass.ds(e, 1)].rearrange("e (k p) n -> p (e k) n", p=P)).then_inc(o_loaded, 16)
                    sp.dma_start(wu, g.dram["moe_w_up"][layer, bass.ds(e, 1)].rearrange("e (k p) n -> p (e k) n", p=P)).then_inc(o_loaded, 16)
                    sp.dma_start(wd, g.dram["moe_w_down"][layer, bass.ds(e, 1)].rearrange("e (k p) n -> p (e k) n", p=P)).then_inc(o_loaded, 16)
                    sp.wait_ge(y_half0, NE + 1 + j)
                    sp.wait_ge(y_half1, NE + 1 + j)
                    sp.dma_start(y_dram[bass.ds((NE + j) * P, P), :], y[:, 0, :]).then_inc(y_stored[0], 16)
            if after:
                for i in range(T):
                    sp.wait_ge(f_out, i + 1)
                    sp.dma_start(g.dram["out"][0, i * P:(i + 1) * P, :], xT[:, i % 2, :, :].rearrange("p k c -> p (k c)")).then_inc(f_stored[i % 2], 16)
                for u in range(2):
                    sp.wait_ge(f_stored[u], 16 * T // 2)

        @block.gpsimd
        def _(pool):
            pool.memset(ones_b[:, :], 1.0).then_inc(consts, 1)
            pool.memset(tri_b[:, :], 1.0).then_inc(consts, 1)
            pool.memset(zeros[:, :], 0.0).then_inc(consts, 1)
            pool.iota(pri[:, :], pattern=[[-1, NE]], base=NE, channel_multiplier=0, allow_small_or_imprecise_dtypes=True).then_inc(consts, 1)
            pool.iota(iota[:, :], pattern=[[1, P]], base=0, channel_multiplier=0, allow_small_or_imprecise_dtypes=True).then_inc(consts, 1)
            pool.iota(tokid[:, :], pattern=[[P, T]], base=0, channel_multiplier=1, allow_small_or_imprecise_dtypes=True).then_inc(consts, 1)
            pool.iota(cap1[:, :], pattern=[[P, NE]], base=0, channel_multiplier=0, allow_small_or_imprecise_dtypes=True).then_inc(consts, 1)
            pool.wait_ge(consts, 7)
            pool.affine_select(out=tri_b[:, :], in_=tri_b[:, :], compare_op=ALU.is_gt, fill=0.0, base=0,
                               pattern=[[1, P]], channel_multiplier=-1).then_inc(consts, 1)
            pool.wait_ge(lists_ready, 1)
            for u in range(2):
                pool.wait_ge(hr_stored[u], 16 * T // 2)

            def gather(e, u, arrived):
                pool.indirect_dma_start(xg[:, u, :], None, hr_dram[:, :],
                                        bass.IndirectOffsetOnAxis(ap=toku[:, e:e + 1], axis=0)).then_inc(arrived, 16)

            for e in range(NE):
                if e >= 2:
                    pool.wait_ge(x_turned, e - 1)
                gather(e, e % 2, xg_loaded[e % 2])
            n_over = over_loop(pool)
            for j in range(NOVER):
                with pool.If(n_over > j):
                    pool.wait_ge(x_turned, NE + j)
                    gather(NE + j, 0, o_gathered)
            for u in range(2):
                pool.wait_ge(y_stored[u], 16 * NE // 2)
            with pool.If(n_over > 0):
                pool.wait_ge(y_stored[0], n_over * 16 + 16 * (NE // 2))
            pool.wait_ge(x_turned, NE)
            for i in range(T):
                if i >= 2:
                    pool.wait_ge(combined, 2 * (i - 1))
                for a, buf in ((0, xg), (1, hr)):
                    pool.indirect_dma_start(buf[:, i % 2, :], None, y_dram[:, :],
                                            bass.IndirectOffsetOnAxis(ap=slotu[:, a * T + i:a * T + i + 1], axis=0)).then_inc(r_loaded[i % 2], 16)

        @block.scalar
        def _(act):
            act.dma_start(wr[:, :, 0:NG], g.dram["moe_w_group"][layer].rearrange("(k p) n -> p k n", p=P)).then_inc(small_loaded, 16)
            act.dma_start(wr[:, :, NG:NR], g.dram["moe_w_router"][layer].rearrange("(k p) n -> p k n", p=P)).then_inc(small_loaded, 16)
            act.dma_start(rbias[:, 0:NG], g.dram["moe_b_group"][layer].partition_broadcast(P)).then_inc(small_loaded, 16)
            act.dma_start(rbias[:, NG:NR], g.dram["moe_b_router"][layer].partition_broadcast(P)).then_inc(small_loaded, 16)

            if after:
                act.dma_start(final_g[:, :], g.dram["final_norm_g"].partition_broadcast(P)).then_inc(final_loaded, 16)

            def square(i):
                if i >= 1:
                    act.wait_ge(squared, i)
                act.activation(sq[:, :], h[:, i, :], ACT.Square, accum_out=ssum[:, i:i + 1]).then_inc(squared, 1)

            square(0)
            for i in range(T):
                if i + 1 < T:
                    square(i + 1)
                act.wait_ge(meaned, i + 1)
                act.activation(rms[:, i:i + 1], ssum[:, i:i + 1], ACT.Sqrt).then_inc(rooted, 1)
            act.wait_ge(ebias, 1)
            act.activation(ga[:, :, :], ga[:, :, :], ACT.Exp).then_inc(expd, 1)
            act.wait_ge(ebias, 2)
            act.activation(small[:, 5, :], small[:, 4, :], ACT.Exp).then_inc(expd, 1)

            def silu(e):
                act.wait_ge(gu_done, e + 1)
                act.activation(sg[:, :], ps[:, GATE, :], ACT.Silu).then_inc(silu_done, 1)

            def copy_hbT(e):
                act.wait_ge(h_turned, e + 1)
                act.activation(hbT[:, :, :], ps[:, HT, :].rearrange("p (k c) -> p k c", c=P), ACT.Copy).then_inc(hbT_ready, 1)

            def copy_y(e, u):
                act.wait_ge(down_done, e + 1)
                act.activation(y[:, u, 0:HALF], ps[:, DOWN[0], :], ACT.Copy).then_inc(y_half0, 1)

            def block_steps(e, u, stored):
                act.wait_ge(hb_ready, e)
                silu(e)
                if stored is not None:
                    act.wait_ge(y_stored[1 - u], 16 * stored)
                copy_y(e - 1, 1 - u)
                copy_hbT(e)

            silu(0)
            copy_hbT(0)
            for e in (1, 2):
                block_steps(e, e % 2, None)
            block_steps(3, 1, 1)
            with act.Fori(2, NE // 2) as i:
                block_steps(2 * i, 0, i - 1)
                block_steps(2 * i + 1, 1, i)
            act.wait_ge(y_stored[1], 16 * (NE // 2 - 1))
            copy_y(NE - 1, 1)
            n_over = over_loop(act)
            with act.If(n_over > 0):
                for u in range(2):
                    act.wait_ge(y_stored[u], 16 * NE // 2)
                with act.Fori(0, n_over) as j:
                    act.wait_ge(o_loaded, j * 48 + 48)
                    act.wait_ge(hb_ready, j + NE)
                    act.wait_ge(gu_done, j + NE + 1)
                    act.activation(sg[:, :], ps[:, GATE, :], ACT.Silu).then_inc(silu_done, 1)
                    act.wait_ge(h_turned, j + NE + 1)
                    act.activation(hbT[:, :, :], ps[:, HT, :].rearrange("p (k c) -> p k c", c=P), ACT.Copy).then_inc(hbT_ready, 1)
                    act.wait_ge(down_done, j + NE + 1)
                    act.activation(y[:, 0, 0:HALF], ps[:, DOWN[0], :], ACT.Copy).then_inc(y_half0, 1)
            if after:
                for i in range(T):
                    act.wait_ge(combined, 2 * i + 2)
                    if i >= 1:
                        act.wait_ge(f_sq, i)
                    act.activation(sq[:, :], h[:, i, :], ACT.Square, accum_out=ssum[:, i:i + 1]).then_inc(f_sq, 1)
                    act.wait_ge(f_mean, i + 1)
                    act.activation(rms[:, i:i + 1], ssum[:, i:i + 1], ACT.Sqrt).then_inc(f_root, 1)

        @block.tensor
        def _(pe):
            pe.wait_ge(small_loaded, 64)
            pe.wait_ge(consts, 8)

            def turn_rows(src):
                for k in range(KT):
                    last = pe.transpose(turn_ps()[:, k, :], src[:, k * P:(k + 1) * P], ident[:, :])
                return last

            for i in range(T):
                pe.wait_ge(hr_ready, i + 1)
                if i >= 1:
                    pe.wait_ge(hnT_ready, i)
                turn_rows(hr[:, i % 2, :]).then_inc(turned, 1)
                if i >= 1:
                    for k in range(KT):
                        last = pe.matmul(ps[:, ROUTE, (i - 1) * NR:i * NR], hnT[:, (i - 1) % 2, k, :], wr[:, k, :],
                                         start=(k == 0), stop=(k == KT - 1))
                    last.then_inc(routed, 1)
            pe.wait_ge(hnT_ready, T)
            for k in range(KT):
                last = pe.matmul(ps[:, ROUTE, (T - 1) * NR:T * NR], hnT[:, (T - 1) % 2, k, :], wr[:, k, :],
                                 start=(k == 0), stop=(k == KT - 1))
            last.then_inc(routed, 1)
            pe.wait_ge(ohb_ready, 1)
            for i in range(T):
                for j in range(i):
                    pe.matmul(ps[:, RANK, i * NE:(i + 1) * NE], ones_b[:, :], ohb[:, j, :], start=(j == 0), stop=False)
                pe.matmul(ps[:, RANK, i * NE:(i + 1) * NE], tri_b[:, :], ohb[:, i, :], start=(i == 0), stop=True)
            for j in range(T):
                last = pe.matmul(ps[:, RANK, T * NE:(T + 1) * NE], ones_b[:, :], ohb[:, j, :], start=(j == 0), stop=(j == T - 1))
            last.then_inc(ranked, 1)
            pe.wait_ge(ab_ready, 1)
            for n in range(2 * T):
                last = pe.matmul(ps[:, ROUTE, 0:NBLK], Am[:, n, :], Bm[:, n, :], start=(n == 0), stop=(n == 2 * T - 1))
            last.then_inc(listed, 1)

            def turn_x(e, u, arrived, count):
                pe.wait_ge(arrived, count)
                pe.wait_ge(xT_ready, e)
                turn_rows(xg[:, u, :]).then_inc(x_turned, 1)

            def gate_up(e, u, w):
                pe.wait_ge(xT_ready, e + 1)
                for b, wm in ((GATE, w[0]), (UP, w[1])):
                    for k in range(KT):
                        last = pe.matmul(ps[:, b, :], xT[:, u, k, :], wm[:, k, :], start=(k == 0), stop=(k == KT - 1))
                last.then_inc(gu_done, 1)

            def turn_h(e):
                pe.wait_ge(hb_ready, e + 1)
                for k in range(ET):
                    last = pe.transpose(ps[:, HT, k * P:(k + 1) * P], hb[:, k * P:(k + 1) * P], ident[:, :])
                last.then_inc(h_turned, 1)

            def down(e, w):
                pe.wait_ge(hbT_ready, e + 1)
                for b in range(2):
                    for k in range(ET):
                        last = pe.matmul(ps[:, DOWN[b], :], hbT[:, k, :], w[2][:, k, b * HALF:(b + 1) * HALF],
                                         start=(k == 0), stop=(k == ET - 1))
                last.then_inc(down_done, 1)

            W = [expert_weights(ring, u) for u in range(2)]
            def block_pair(i, last):
                pe.wait_ge(gu_loaded[0], 32 * i + 32)
                gate_up(2 * i, 0, W[0])
                turn_x(2 * i + 1, 1, xg_loaded[1], 16 * i + 16)
                pe.wait_ge(down_loaded[1], 16 * i)
                pe.wait_ge(y_half0, 2 * i - 1)
                pe.wait_ge(y_half1, 2 * i - 1)
                down(2 * i - 1, W[1])
                turn_h(2 * i)
                pe.wait_ge(gu_loaded[1], 32 * i + 32)
                gate_up(2 * i + 1, 1, W[1])
                if not last:
                    turn_x(2 * i + 2, 0, xg_loaded[0], 16 * i + 32)
                pe.wait_ge(down_loaded[0], 16 * i + 16)
                pe.wait_ge(y_half0, 2 * i)
                pe.wait_ge(y_half1, 2 * i)
                down(2 * i, W[0])
                turn_h(2 * i + 1)

            pe.wait_ge(xg_loaded[0], 16)
            pe.wait_ge(lists_ready, 1)
            turn_rows(xg[:, 0, :]).then_inc(x_turned, 1)
            pe.wait_ge(gu_loaded[0], 32)
            gate_up(0, 0, W[0])
            turn_x(1, 1, xg_loaded[1], 16)
            turn_h(0)
            pe.wait_ge(gu_loaded[1], 32)
            gate_up(1, 1, W[1])
            turn_x(2, 0, xg_loaded[0], 32)
            pe.wait_ge(down_loaded[0], 16)
            down(0, W[0])
            turn_h(1)
            with pe.Fori(1, NE // 2 - 1) as i:
                block_pair(i, False)
            block_pair(NE // 2 - 1, True)
            pe.wait_ge(down_loaded[1], 16 * (NE // 2))
            pe.wait_ge(y_half0, NE - 1)
            pe.wait_ge(y_half1, NE - 1)
            down(NE - 1, W[1])
            n_over = over_loop(pe)
            with pe.If(n_over > 0):
                with pe.Fori(0, n_over) as j:
                    e = j + NE
                    turn_x(e, 0, o_gathered, j * 16 + 16)
                    pe.wait_ge(o_loaded, j * 48 + 48)
                    gate_up(e, 0, W[0])
                    turn_h(e)
                    pe.wait_ge(y_half0, e)
                    pe.wait_ge(y_half1, e)
                    down(e, W[0])

        @block.vector
        def _(dve):
            count = [0]

            def chain(ins):
                count[0] += 1
                ins.then_inc(step, 1)
                dve.wait_ge(step, count[0])

            def tt(out, a, b, op):
                chain(dve.tensor_tensor(out, a, b, op))

            def ts(out, a, s1, s2, op0, op1=ALU.bypass):
                chain(dve.tensor_scalar(out, a, s1, s2, op0, op1))

            def evacuate(i):
                dve.wait_ge(turned, i + 1)
                if i >= 2:
                    dve.wait_ge(routed, i - 1)
                dve.tensor_tensor(hnT[:, i % 2, :, :], turn_ps(), gcol.unsqueeze(2).to_broadcast([P, KT, P]),
                                  ALU.mult).then_inc(hnT_ready, 1)

            dve.wait_ge(small_loaded, 64)
            for i in range(T):
                dve.wait_ge(squared, i + 1)
                dve.tensor_scalar(ssum[:, i:i + 1], ssum[:, i:i + 1], 1.0 / D, EPS, ALU.mult, ALU.add).then_inc(meaned, 1)
                if i >= 1:
                    evacuate(i - 1)
                dve.wait_ge(rooted, i + 1)
                chain(dve.reciprocal(rinv[:, i:i + 1], rms[:, i:i + 1]))
                if i >= 2:
                    dve.wait_ge(hr_stored[i % 2], 16 * (i // 2))
                dve.tensor_scalar(hr[:, i % 2, :], h[:, i, :], rinv[:, i:i + 1], None, ALU.mult).then_inc(hr_ready, 1)
            evacuate(T - 1)

            dve.wait_ge(routed, T)
            dve.wait_ge(consts, 8)
            psR = ps[:, ROUTE, 0:T * NR].rearrange("p (t n) -> p t n", t=T)
            tt(lg[:, :, :], psR, rbias[:, :].unsqueeze(1).to_broadcast([P, T, NR]), ALU.add)
            gl, el = lg[:, :, 0:NG], lg[:, :, NG:NR]
            gmax, gp, gsum, ggate, diff, ed, m1, m2, p1, den = (small[:, n, :] for n in (0, 1, 2, 3, 4, 5, 6, 7, 8, 9))

            def bc(v, n):
                return v.unsqueeze(2).to_broadcast([P, T, n])

            def first_best(out, values, best, prio, pbest, tmp, n):
                chain(dve.tensor_reduce(best, values, AX.X, ALU.max))
                tt(tmp, values, bc(best, n), ALU.is_equal)
                tt(tmp, tmp, prio.unsqueeze(1).to_broadcast([P, T, n]), ALU.mult)
                chain(dve.tensor_reduce(pbest, tmp, AX.X, ALU.max))
                tt(out, tmp, bc(pbest, n), ALU.is_equal)

            first_best(goh[:, :, :], gl, gmax, pri[:, 0:NG], gp, ga[:, :, :], NG)
            dve.tensor_tensor(ga[:, :, :], gl, bc(gmax, NG), ALU.subtract).then_inc(ebias, 1)
            ts(slotm[:, :, 0:NG], goh[:, :, :], NEG, -NEG, ALU.mult, ALU.add)
            for t in range(T):
                last = dve.tensor_tensor(em[:, t, :].rearrange("p (g n) -> p g n", g=NG),
                                         lg[:, t, NG:NR].rearrange("p (g n) -> p g n", g=NG),
                                         slotm[:, t, 0:NG].unsqueeze(2).to_broadcast([P, NG, NPG]), ALU.add)
            chain(last)
            first_best(oh[:, 0, :, :], em[:, :, :], m1, pri[:, :], p1, ea[:, :, :], NE)
            chain(dve.scalar_tensor_tensor(em[:, :, :], oh[:, 0, :, :], -2 * NEG, em[:, :, :], ALU.mult, ALU.add))
            first_best(oh[:, 1, :, :], em[:, :, :], m2, pri[:, :], p1, ea[:, :, :], NE)
            dve.tensor_tensor(diff, m2, m1, ALU.subtract).then_inc(ebias, 1)
            dve.tensor_tensor(ohb[:, :, :], oh[:, 0, :, :], oh[:, 1, :, :], ALU.add).then_inc(ohb_ready, 1)
            dve.wait_ge(expd, 2)
            chain(dve.tensor_reduce(gsum, ga[:, :, :], AX.X, ALU.add))
            chain(dve.reciprocal(ggate, gsum))
            ts(den, ed, 1.0, None, ALU.add)
            chain(dve.reciprocal(p1, den))
            tt(wts[:, 0, :], p1, ggate, ALU.mult)
            tt(wts[:, 1, :], wts[:, 0, :], ed, ALU.mult)
            dve.wait_ge(ranked, 1)
            psK = ps[:, RANK, 0:T * NE].rearrange("p (t n) -> p t n", t=T)
            ts(novi[:, :], ps[:, RANK, T * NE:(T + 1) * NE], float(P - 1), None, ALU.add)
            ts(novi[:, :], novi[:, :], 7, None, ALU.arith_shift_right)
            chain(dve.tensor_copy(novf[:, :], novi[:, :]))
            ts(novf[:, :], novf[:, :], -1.0, 0.0, ALU.add, ALU.max)
            chain(dve.tensor_tensor_scan(obend[:, :], novf[:, :], zeros[:, :], 0.0, ALU.add, ALU.add))
            tt(dlt[:, :], obend[:, :], novf[:, :], ALU.subtract)
            ts(dlt[:, :], dlt[:, :], float(P), float((NE - 1) * P), ALU.mult, ALU.add)
            tt(dlt[:, :], dlt[:, :], cap1[:, :], ALU.subtract)
            ts(slotm[:, :, :], psK, float(P), None, ALU.is_ge)
            tt(slotm[:, :, :], slotm[:, :, :], dlt[:, :].unsqueeze(1).to_broadcast([P, T, NE]), ALU.mult)
            tt(slotm[:, :, :], slotm[:, :, :], psK, ALU.add)
            tt(slotm[:, :, :], slotm[:, :, :], cap1[:, :].unsqueeze(1).to_broadcast([P, T, NE]), ALU.add)
            for a in range(2):
                tt(ea[:, :, :], slotm[:, :, :], oh[:, a, :, :], ALU.mult)
                chain(dve.tensor_reduce(slot[:, a, :], ea[:, :, :], AX.X, ALU.add))
            chain(dve.tensor_copy(sloti[:, :, :], slot[:, :, :]))
            chain(dve.tensor_copy(slotu[:, :], slot[:, :, :].rearrange("p a t -> p (a t)")))
            ts(blki[:, :, :], sloti[:, :, :], 7, None, ALU.arith_shift_right)
            ts(loi[:, :, :], sloti[:, :, :], P - 1, None, ALU.bitwise_and)
            chain(dve.tensor_copy(blk[:, :, :], blki[:, :, :]))
            chain(dve.tensor_copy(lo[:, :, :], loi[:, :, :]))
            for u in range(2):
                dve.wait_ge(hr_stored[u], 16 * T // 2)
            for a in range(2):
                for t in range(T):
                    dve.tensor_scalar(Am[:, a * T + t, :], iota[:, :], lo[:, a, t:t + 1], None, ALU.is_equal)
                    last = dve.tensor_scalar(Bm[:, a * T + t, :], iota[:, 0:NBLK], blk[:, a, t:t + 1], tokid[:, t:t + 1],
                                             ALU.is_equal, ALU.mult)
            last.then_inc(ab_ready, 1)
            tt(eidc[:, :, :], obend[:, :].unsqueeze(1).to_broadcast([P, NOVER, NE]),
               iota[:, 0:NOVER].unsqueeze(2).to_broadcast([P, NOVER, NE]), ALU.is_le)
            chain(dve.tensor_reduce(eid[:, :], eidc[:, :, :], AX.X, ALU.add))
            chain(dve.tensor_copy(eidi[:, 0:NOVER], eid[:, :]))
            chain(dve.tensor_copy(eidi[:, NOVER:NOVER + 1], obend[:, NE - 1:NE]))
            dve.wait_ge(listed, 1)
            dve.tensor_copy(toku[:, :], ps[:, ROUTE, 0:NBLK]).then_inc(lists_ready, 1)

            def copy_xT(e, u):
                dve.wait_ge(x_turned, e + 1)
                dve.tensor_tensor(xT[:, u, :, :], turn_ps(), gcol.unsqueeze(2).to_broadcast([P, KT, P]),
                                  ALU.mult).then_inc(xT_ready, 1)

            def product(e):
                dve.wait_ge(silu_done, e + 1)
                dve.tensor_tensor(hb[:, :], sg[:, :], ps[:, UP, :], ALU.mult).then_inc(hb_ready, 1)

            def copy_y(e, u):
                dve.wait_ge(down_done, e + 1)
                dve.tensor_copy(y[:, u, HALF:D], ps[:, DOWN[1], :]).then_inc(y_half1, 1)

            def block_steps(e, u, stored, last=False):
                dve.wait_ge(h_turned, e)
                product(e)
                if not last:
                    dve.wait_ge(gu_done, e)
                    copy_xT(e + 1, 1 - u)
                if stored is not None:
                    dve.wait_ge(y_stored[1 - u], 16 * stored)
                copy_y(e - 1, 1 - u)

            copy_xT(0, 0)
            product(0)
            copy_xT(1, 1)
            for e in (1, 2):
                block_steps(e, e % 2, None)
            block_steps(3, 1, 1)
            with dve.Fori(2, NE // 2 - 1) as i:
                block_steps(2 * i, 0, i - 1)
                block_steps(2 * i + 1, 1, i)
            block_steps(NE - 2, 0, NE // 2 - 2)
            block_steps(NE - 1, 1, NE // 2 - 1, last=True)
            dve.wait_ge(y_stored[1], 16 * (NE // 2 - 1))
            copy_y(NE - 1, 1)
            n_over = over_loop(dve)
            with dve.If(n_over > 0):
                for u in range(2):
                    dve.wait_ge(y_stored[u], 16 * NE // 2)
                with dve.Fori(0, n_over) as j:
                    e = j + NE
                    dve.wait_ge(o_loaded, j * 48 + 48)
                    dve.wait_ge(gu_done, e)
                    copy_xT(e, 0)
                    dve.wait_ge(h_turned, e)
                    product(e)
                    dve.wait_ge(down_done, e + 1)
                    dve.tensor_copy(y[:, 0, HALF:D], ps[:, DOWN[1], :]).then_inc(y_half1, 1)

            for i in range(T):
                dve.wait_ge(r_loaded[i % 2], 32 * (i // 2 + 1))
                dve.scalar_tensor_tensor(h[:, i, :], xg[:, i % 2, :], wts[:, 0, i:i + 1], h[:, i, :],
                                         ALU.mult, ALU.add).then_inc(combined, 1)
                dve.wait_ge(combined, 2 * i + 1)
                dve.scalar_tensor_tensor(h[:, i, :], hr[:, i % 2, :], wts[:, 1, i:i + 1], h[:, i, :],
                                         ALU.mult, ALU.add).then_inc(combined, 1)
                if after:
                    dve.wait_ge(f_sq, i + 1)
                    dve.tensor_scalar(ssum[:, i:i + 1], ssum[:, i:i + 1], 1.0 / D, EPS, ALU.mult, ALU.add).then_inc(f_mean, 1)
                    dve.wait_ge(f_root, i + 1)
                    chain(dve.reciprocal(rinv[:, i:i + 1], rms[:, i:i + 1]))
                    if i == 0:
                        dve.wait_ge(final_loaded, 16)
                    if i >= 2:
                        dve.wait_ge(f_stored[i % 2], 16 * (i // 2))
                    dve.scalar_tensor_tensor(xT[:, i % 2, :, :].rearrange("p k c -> p (k c)"), h[:, i, :], rinv[:, i:i + 1],
                                             final_g[:, :], ALU.mult, ALU.mult).then_inc(f_out, 1)


def setup(nc, g, ctx, arrays):
    g.of_block = []
    g.dram = arrays
    g.h = ctx.enter_context(nc.sbuf_tensor("h", [P, T, D], F32))
    g.ring = ctx.enter_context(nc.sbuf_tensor("ring", [P, 2 * SLOT], F32))
    g.ident = ctx.enter_context(nc.sbuf_tensor("ident", [P, P], F32))
    g.mean_w = ctx.enter_context(nc.sbuf_tensor("mean_w", [P, P], F32))
    g.vecs = ctx.enter_context(nc.sbuf_tensor("vecs", [P, V_ROWS], F32))
    g.ps = ctx.enter_context(nc.psum_tensor("ps", [P, 8, HALF], F32))
    g.y_dram = nc.dram_tensor("y_dram", [NBLK * P, D], F32, kind="Internal").ap()
    g.gu_loaded = [[ctx.enter_context(nc.semaphore(f"gu_loaded{n}{u}")) for u in range(2)] for n in range(2)]
    g.down_loaded = [[ctx.enter_context(nc.semaphore(f"down_loaded{n}{u}")) for u in range(2)] for n in range(2)]


def hybrid_kernel(nc, arrays):
    with ExitStack() as ctx:
        g = Shared()
        setup(nc, g, ctx, arrays)
        conv_block(nc, g)
        g.end_block(nc)
        moe_block(nc, g, 0, False)
        g.end_block(nc)
        attention_block(nc, g)
        g.end_block(nc)
        moe_block(nc, g, 1, True)


def rope_tables():
    import numpy as np
    inv = np.float32(ROPE_THETA) ** (-np.arange(0, ROT, 2, dtype=np.float32) / np.float32(ROT))
    ang = np.arange(S, dtype=np.float32)[:, None] * inv.astype(np.float32)[None, :]
    return np.stack([np.cos(ang), np.sin(ang)]).astype(np.float32)


_INS = ['x', 'mix_norm_g', 'ffn_norm_g', 'final_norm_g', 'conv_w_in', 'conv_b_in', 'conv_w_dw', 'conv_b_dw', 'conv_ln_g',
        'conv_ln_b', 'conv_w_out', 'conv_b_out', 'attn_w_in', 'idx_k_ln_g', 'idx_k_ln_b', 'attn_w_out', 'moe_w_group',
        'moe_b_group', 'moe_w_router', 'moe_b_router', 'moe_w_gate', 'moe_w_up', 'moe_w_down']


def kernel(**inputs):
    import numpy as np
    import concourse.bacc as bacc
    from concourse.bass_utils import run_bass_kernel_spmd

    nc = bacc.Bacc("TRN2", target_bir_lowering=False, num_devices=1)
    given = {name: np.ascontiguousarray(inputs[name]) for name in _INS}
    given["rope"] = rope_tables()
    arrays = {}
    for name, a in given.items():
        arrays[name] = nc.dram_tensor(f"in_{name}_dram", a.shape, mybir.dt.from_np(a.dtype), kind="ExternalInput").ap()
    arrays["out"] = nc.dram_tensor("out_dram", (1, S, D), F32, kind="ExternalOutput").ap()
    hybrid_kernel(nc, arrays)
    r = run_bass_kernel_spmd(nc, [{f"in_{name}_dram": a for name, a in given.items()}], core_ids=[0])
    return r.results[0]["out_dram"]
```

```python
from contextlib import ExitStack

import concourse.bass as bass
from concourse import mybir

F32 = mybir.dt.float32
F32R = mybir.dt.float32r
BF16 = mybir.dt.bfloat16
I32 = mybir.dt.int32
U32 = mybir.dt.uint32
ALU = mybir.AluOpType
ACT = mybir.ActivationFunctionType
AX = mybir.AxisListType

P = 128
S = 1024
D = 1024
T = S // P
KT = D // P
HALF = 512
EPS = 1e-6
CW = 31
H, NKV, HD = 16, 4, 64
IH = 8
QC, KVC = H * HD, NKV * HD
ROT = HD // 4
CHUNK = 64
TOPK = 256
ROPE_THETA = 500000.0
INADMISSIBLE, TAKEN = -1e38, -3e38
NG, NPG = 4, 8
NE = NG * NPG
DE = 512
ET = DE // P
NR = NG + NE
TOPE = 2
NOVER = (S * TOPE) // (P + 1)
NBLK = NE + NOVER
NEG = 1e30
WG, WU, WD = 0, KT * DE, 2 * KT * DE
SLOT = 2 * KT * DE + ET * D
GATE_PIECES = KT * DE // D
GU_PIECES = 2 * GATE_PIECES
NPIECE = GU_PIECES + ET
AHEAD = 8
EARLY = 5
ROWBUFS = 4
AT = (ET, 0)

V_MIX, V_FFN, V_BIN, V_BDW, V_LNG, V_LNB, V_ROWS = 0, 16, 32, 48, 56, 64, 72


class Shared:

    def semaphore(self, nc, name):
        self.of_block.append(nc.alloc_semaphore(name=name))
        return self.of_block[-1]

    def end_block(self, nc):
        nc.clear_and_free_semaphores(self.of_block)
        self.of_block = []
        nc.all_engine_barrier()


def expert_weights(ring, slot):
    w = ring[:, slot * SLOT:(slot + 1) * SLOT]
    return (w[:, WG:WU].rearrange("p (k n) -> p k n", k=KT),
            w[:, WU:WD].rearrange("p (k n) -> p k n", k=KT),
            w[:, WD:SLOT].rearrange("p (k n) -> p k n", k=ET))


def split_product(pe, out, a_high, a_low, b_high, b_low, start, stop):
    pe.matmul(out, a_high, b_high, start=start, stop=False)
    pe.matmul(out, a_high, b_low, start=False, stop=False)
    return pe.matmul(out, a_low, b_high, start=False, stop=stop)


def conv_block(nc, g):
    with ExitStack() as ctx:
        def sb(name, shape, dt=F32):
            return ctx.enter_context(nc.sbuf_tensor("c_" + name, shape, dt))

        def sem(name):
            return g.semaphore(nc, "c_" + name)

        h, ring, ps, ident, vecs = g.h, g.ring, g.ps, g.ident, g.vecs
        PAD = CW - 1
        w_in = ring[:, 0:2 * KT * D].rearrange("p (f s k n) -> p f s k n", f=KT, s=2, k=KT)
        w_out = ring[:, 2 * KT * D:3 * KT * D].rearrange("p (k n) -> p k n", k=KT)

        hnT = sb("hnT", [P, KT, S])
        cT = sb("cT", [P, KT, S])
        c_high = nc.alloc_sbuf_tensor_at("c_c_high", [P, KT, S], F32R, offset=nc.sbuf_base - 4 * 2 * KT * S)
        c_low = nc.alloc_sbuf_tensor_at("c_c_low", [P, KT, S], F32R, offset=nc.sbuf_base - 4 * KT * S)
        wout_high = nc.alloc_sbuf_tensor_at("c_wout_high", [P, KT, D], F32R, offset=g.ring_at + 4 * 2 * S)
        wout_low = nc.alloc_sbuf_tensor_at("c_wout_low", [P, KT, D], F32R, offset=g.ring_at + 4 * 2 * KT * D)
        upad = sb("upad", [P, 2, PAD + S])
        scratch = sb("scratch", [P, 2, HALF])
        vrows = sb("vrows", [V_ROWS, P])
        taps = sb("taps", [P, KT, 32])
        ssum = sb("ssum", [P, T]); rms = sb("rms", [P, T]); rinv = sb("rinv", [P, T])
        wrows = upad[0:CW, 0, 0:D]
        hr = cT[:, 0:2, :]
        tapped = [ring[:, n * S:(n + 1) * S] for n in range(2)]
        part = [cT[:, f + 1, :] for f in range(KT - 1)] + [upad[:, 0, 0:S]]
        rstd = upad[:, 0, 0:S]
        bout = upad[:, 1, 0:D]

        x_loaded = [sem(f"x_loaded{i}") for i in range(T)]
        win_loaded = [sem(f"win_loaded{f}") for f in range(KT)]
        wout_loaded = sem("wout_loaded"); vec_loaded = sem("vec_loaded"); fill = sem("fill")
        made = sem("made"); vec_turned = sem("vec_turned"); vec_ready = sem("vec_ready")
        squared = sem("squared"); meaned = sem("meaned"); rooted = sem("rooted"); step = sem("step")
        hr_ready = sem("hr_ready"); turned = sem("turned"); hnT_ready = sem("hnT_ready")
        gated = sem("gated"); unit_done = sem("unit_done"); u_ready = sem("u_ready"); conv_done = sem("conv_done")
        padded = sem("padded"); part_step = sem("part_step"); tap_ready = sem("tap_ready"); w_high = sem("w_high"); w_low = sem("w_low")
        act_high = sem("act_high"); act_low = sem("act_low"); summed = sem("summed"); centred = sem("centred"); sq_ready = sem("sq_ready")
        var_done = sem("var_done"); var_eps = sem("var_eps"); dev = sem("dev"); scaled = sem("scaled")
        activated = sem("activated"); out_done = sem("out_done"); h_ready = sem("h_ready"); bout_loaded = sem("bout_loaded")

        SIDE_TAPS = 11
        NU = 2 * KT

        def banks(n):
            return 2 * (n % 3), 2 * (n % 3) + 1

        MEAN, VAR, OUT = (6, 7), (0, 1), ((2, 3), (4, 5))

        block = ctx.enter_context(nc.Block())

        @block.sync
        def _(sp):
            for i in range(T):
                sp.dma_start(h[:, i, :], g.dram["x"][0, i * P:(i + 1) * P, :]).then_inc(x_loaded[i], 16)
            for f in range(KT):
                for s in range(2):
                    sp.dma_start(w_in[:, f, s, :, :],
                                 g.dram["conv_w_in"][0].rearrange("(k p) n -> p k n", p=P)[:, :, s * D + f * P:s * D + (f + 1) * P]).then_inc(win_loaded[f], 16)
            sp.dma_start(w_out, g.dram["conv_w_out"][0].rearrange("(k p) n -> p k n", p=P)).then_inc(wout_loaded, 16)
            for j in range(NE, NBLK):
                sp.dma_start(g.y_dram[j * P:(j + 1) * P, :], g.dram["x"][0, 0:P, :]).then_inc(fill, 16)
            sp.wait_ge(conv_done, KT)
            sp.dma_start(bout, g.dram["conv_b_out"][0].partition_broadcast(P)).then_inc(bout_loaded, 16)
            sp.wait_ge(fill, 16 * NOVER)

        @block.gpsimd
        def _(pool):
            pool.memset(ident[:, :], 0.0).then_inc(made, 1)
            pool.memset(g.mean_w[:, :], 1.0 / D).then_inc(made, 1)
            pool.wait_ge(made, 2)
            pool.affine_select(out=ident[:, :], in_=ident[:, :], compare_op=ALU.not_equal, fill=1.0, base=0,
                               pattern=[[-1, P]], channel_multiplier=1).then_inc(made, 1)
            pool.wait_ge(vec_ready, 2)
            pool.memset(upad[:, :, 0:PAD], 0.0).then_inc(padded, 1)
            for f in range(KT):
                for j in range(1, SIDE_TAPS):
                    n = (SIDE_TAPS - 1) * f + j - 1
                    pool.wait_ge(tap_ready, n + f + 2)
                    if n >= 1:
                        pool.wait_ge(part_step, n)
                    pool.tensor_tensor(part[f], part[f], tapped[n % 2], ALU.add).then_inc(part_step, 1)
                if f >= 4:
                    for k in (2 * (f - 4), 2 * (f - 4) + 1):
                        pool.wait_ge(w_high, k + 1)
                        pool.tensor_tensor(wout_low[:, k, :], w_out[:, k, :], wout_high[:, k, :].bitcast(F32), ALU.subtract).then_inc(w_low, 1)

        @block.scalar
        def _(act):
            for row, src in ((V_MIX, g.dram["mix_norm_g"]), (V_FFN, g.dram["ffn_norm_g"]), (V_BIN, g.dram["conv_b_in"]), (V_BDW, g.dram["conv_b_dw"]),
                             (V_LNG, g.dram["conv_ln_g"]), (V_LNB, g.dram["conv_ln_b"])):
                n = src.shape[0] * src.shape[1] // P
                act.dma_start(vrows[row:row + n, :], src.rearrange("l (r c) -> (l r) c", c=P)).then_inc(vec_loaded, 16)
            act.dma_start(wrows, g.dram["conv_w_dw"][0]).then_inc(vec_loaded, 16)
            sq = scratch[:, :, :].rearrange("p a b -> p (a b)")

            def square(i):
                act.wait_ge(x_loaded[i], 16)
                if i >= 1:
                    act.wait_ge(squared, i)
                act.activation(sq, h[:, i, :], ACT.Square, accum_out=ssum[:, i:i + 1]).then_inc(squared, 1)

            square(0)
            for i in range(T):
                if i + 1 < T:
                    square(i + 1)
                act.wait_ge(meaned, i + 1)
                act.activation(rms[:, i:i + 1], ssum[:, i:i + 1], ACT.Sqrt).then_inc(rooted, 1)

            def sigmoid(n):
                act.wait_ge(unit_done, n + 1)
                if n >= 2:
                    act.wait_ge(u_ready, n - 1)
                act.activation(scratch[:, n % 2, :], ps[:, banks(n)[1], :], ACT.Sigmoid,
                               bias=vecs[:, V_BIN + KT + n // 2:V_BIN + KT + n // 2 + 1]).then_inc(gated, 1)
                if n >= 8:
                    k = n - 8
                    if k == 0:
                        act.wait_ge(wout_loaded, 16)
                    act.activation(wout_high[:, k, :], w_out[:, k, :], ACT.Copy).then_inc(w_high, 1)

            def tap(f, j):
                n = (SIDE_TAPS - 1) * f + j - 1
                if j >= 1 and n >= 2:
                    act.wait_ge(part_step, n - 1)
                act.activation(tapped[n % 2] if j >= 1 else part[f], upad[:, f % 2, j:j + S], ACT.Copy,
                               scale=taps[:, f, j:j + 1]).then_inc(tap_ready, 1)

            sigmoid(0)
            sigmoid(1)
            act.wait_ge(padded, 1)
            for f in range(KT):
                act.wait_ge(u_ready, 2 * f + 2)
                if f == KT - 1:
                    act.wait_ge(conv_done, f)
                for j in range(SIDE_TAPS):
                    tap(f, j)
                    if f + 1 < KT and j in (SIDE_TAPS // 2, SIDE_TAPS - 1):
                        sigmoid(2 * f + (2 if j < SIDE_TAPS - 1 else 3))
            for n in range(NU):
                f, half = n % KT, n // KT
                act.wait_ge(centred, n + 1)
                act.activation(hnT[:, f, half * HALF:(half + 1) * HALF], cT[:, f, half * HALF:(half + 1) * HALF],
                               ACT.Square).then_inc(sq_ready, 1)
            for half in range(2):
                cols = slice(half * HALF, (half + 1) * HALF)
                act.wait_ge(var_eps, half + 1)
                act.activation(rstd[:, cols], rstd[:, cols], ACT.Sqrt).then_inc(dev, 1)
                for f in range(KT):
                    act.wait_ge(scaled, half * KT + f + 1)
                    act.activation(cT[:, f, cols], cT[:, f, cols], ACT.Silu, scale=vecs[:, V_LNG + f:V_LNG + f + 1],
                                   bias=vecs[:, V_LNB + f:V_LNB + f + 1]).then_inc(activated, 1)
                    act.wait_ge(activated, half * KT + f + 1)
                    act.activation(c_high[:, f, cols], cT[:, f, cols], ACT.Copy).then_inc(act_high, 1)
            for i in range(T):
                act.wait_ge(h_ready, i + 1)
                act.wait_ge(squared, T + i)
                act.activation(sq, h[:, i, :], ACT.Square, accum_out=g.ssum[:, i:i + 1]).then_inc(squared, 1)

        @block.tensor
        def _(pe):
            pe.wait_ge(made, 3)
            pe.wait_ge(vec_loaded, 16 * 7)
            pe.transpose(ps[:, 6, 0:V_ROWS], vrows[:, :], ident[0:V_ROWS, 0:V_ROWS]).then_inc(vec_turned, 1)
            for f in range(KT):
                last = pe.transpose(ps[:, 7, 32 * f:32 * f + CW], wrows[:, f * P:(f + 1) * P], ident[0:CW, 0:CW])
            last.then_inc(vec_turned, 1)
            for i in range(T):
                pe.wait_ge(hr_ready, i + 1)
                if i >= 2:
                    pe.wait_ge(hnT_ready, i - 1)
                tps = ps[:, 2 * (i % 2):2 * (i % 2) + 2, :].rearrange("p b (k c) -> p (b k) c", c=P)
                for k in range(KT):
                    last = pe.transpose(tps[:, k, :], hr[:, i % 2, k * P:(k + 1) * P], ident[:, :])
                last.then_inc(turned, 1)

            def mean_of(f):
                pe.wait_ge(conv_done, f + 1)
                for half in range(2):
                    last = pe.matmul(ps[:, MEAN[half], :], g.mean_w[:, :], cT[:, f, half * HALF:(half + 1) * HALF],
                                     start=(f == 0), stop=(f == KT - 1))
                last.then_inc(summed, 1)

            pe.wait_ge(vec_ready, 2)
            for n in range(NU):
                f, half = n // 2, n % 2
                if half == 0:
                    pe.wait_ge(win_loaded[f], 32)
                if n < 2:
                    pe.wait_ge(hnT_ready, T - 1 + n)
                if n >= 3:
                    pe.wait_ge(u_ready, n - 2)
                for s in range(2):
                    for k in range(KT):
                        last = pe.matmul(ps[:, banks(n)[s], :], w_in[:, f, s, k, :], hnT[:, k, half * HALF:(half + 1) * HALF],
                                         start=(k == 0), stop=(k == KT - 1))
                last.then_inc(unit_done, 1)
                if half == 1 and f >= 2:
                    mean_of(f - 2)
            mean_of(KT - 2)
            mean_of(KT - 1)
            for n in range(NU):
                f, half = n % KT, n // KT
                pe.wait_ge(sq_ready, n + 1)
                last = pe.matmul(ps[:, VAR[half], :], g.mean_w[:, :], hnT[:, f, half * HALF:(half + 1) * HALF],
                                 start=(f == 0), stop=(f == KT - 1))
                if f == KT - 1:
                    last.then_inc(var_done, 1)
            pe.wait_ge(w_low, KT)
            for i in range(T):
                pe.wait_ge(act_low, KT * (i // (T // 2) + 1))
                if i >= 2:
                    pe.wait_ge(h_ready, i - 1)
                for b in range(2):
                    for k in range(KT):
                        last = split_product(pe, ps[:, OUT[i % 2][b], :], c_high[:, k, i * P:(i + 1) * P], c_low[:, k, i * P:(i + 1) * P],
                                             wout_high[:, k, b * HALF:(b + 1) * HALF], wout_low[:, k, b * HALF:(b + 1) * HALF],
                                             k == 0, k == KT - 1)
                last.then_inc(out_done, 1)

        @block.vector
        def _(dve):
            count = [0]

            def mark(ins):
                count[0] += 1
                ins.then_inc(step, 1)
                return count[0]

            def after(n):
                dve.wait_ge(step, n)

            dve.wait_ge(vec_turned, 2)
            dve.tensor_copy(vecs[:, :], ps[:, 6, 0:V_ROWS]).then_inc(vec_ready, 1)
            dve.tensor_copy(taps[:, :, 0:CW], ps[:, 7, 0:32 * KT].rearrange("p (f j) -> p f j", f=KT)[:, :, 0:CW]).then_inc(vec_ready, 1)
            dve.wait_ge(vec_ready, 2)
            gcol = vecs[:, V_MIX:V_MIX + KT]

            def evacuate(i):
                dve.wait_ge(turned, i + 1)
                tps = ps[:, 2 * (i % 2):2 * (i % 2) + 2, :].rearrange("p b (k c) -> p (b k) c", c=P)
                dve.tensor_tensor(hnT[:, :, i * P:(i + 1) * P], tps, gcol.unsqueeze(2).to_broadcast([P, KT, P]),
                                  ALU.mult).then_inc(hnT_ready, 1)

            for i in range(T):
                dve.wait_ge(squared, i + 1)
                dve.tensor_scalar(ssum[:, i:i + 1], ssum[:, i:i + 1], 1.0 / D, EPS, ALU.mult, ALU.add).then_inc(meaned, 1)
                if i >= 1:
                    evacuate(i - 1)
                dve.wait_ge(rooted, i + 1)
                after(mark(dve.reciprocal(rinv[:, i:i + 1], rms[:, i:i + 1])))
                dve.tensor_scalar(hr[:, i % 2, :], h[:, i, :], rinv[:, i:i + 1], None, ALU.mult).then_inc(hr_ready, 1)
            evacuate(T - 1)

            dve.wait_ge(padded, 1)
            for f in range(KT):
                for half in range(2):
                    n = 2 * f + half
                    dve.wait_ge(gated, n + 1)
                    dve.scalar_tensor_tensor(upad[:, f % 2, PAD + half * HALF:PAD + (half + 1) * HALF], ps[:, banks(n)[0], :],
                                             vecs[:, V_BIN + f:V_BIN + f + 1], scratch[:, n % 2, :], ALU.add, ALU.mult).then_inc(u_ready, 1)
                dve.wait_ge(u_ready, 2 * f + 2)
                before = [0, 0]
                for j in range(SIDE_TAPS, CW):
                    for half in range(2):
                        cols = slice(half * HALF, (half + 1) * HALF)
                        src = upad[:, f % 2, j + half * HALF:j + (half + 1) * HALF]
                        if j == SIDE_TAPS:
                            before[half] = mark(dve.tensor_scalar(cT[:, f, cols], src, taps[:, f, j:j + 1], vecs[:, V_BDW + f:V_BDW + f + 1],
                                                                  ALU.mult, ALU.add))
                            continue
                        after(before[half])
                        before[half] = mark(dve.scalar_tensor_tensor(cT[:, f, cols], src, taps[:, f, j:j + 1], cT[:, f, cols], ALU.mult, ALU.add))
                dve.wait_ge(part_step, (SIDE_TAPS - 1) * (f + 1))
                after(before[1])
                dve.tensor_tensor(cT[:, f, :], cT[:, f, :], part[f], ALU.add).then_inc(conv_done, 1)

            dve.wait_ge(summed, KT)
            for n in range(NU):
                f, half = n % KT, n // KT
                cols = slice(half * HALF, (half + 1) * HALF)
                dve.scalar_tensor_tensor(cT[:, f, cols], ps[:, MEAN[half], :], -1.0, cT[:, f, cols], ALU.mult, ALU.add).then_inc(centred, 1)
            for half in range(2):
                cols = slice(half * HALF, (half + 1) * HALF)
                dve.wait_ge(var_done, half + 1)
                dve.tensor_scalar(rstd[:, cols], ps[:, VAR[half], :], EPS, None, ALU.add).then_inc(var_eps, 1)
                dve.wait_ge(dev, half + 1)
                after(mark(dve.reciprocal(rstd[:, cols], rstd[:, cols])))
                for f in range(KT + 2):
                    if f < KT:
                        dve.tensor_tensor(cT[:, f, cols], cT[:, f, cols], rstd[:, cols], ALU.mult).then_inc(scaled, 1)
                    if f >= 2:
                        dve.wait_ge(act_high, half * KT + f - 1)
                        dve.tensor_tensor(c_low[:, f - 2, cols], cT[:, f - 2, cols], c_high[:, f - 2, cols].bitcast(F32),
                                          ALU.subtract).then_inc(act_low, 1)

            dve.wait_ge(bout_loaded, 16)
            for i in range(T):
                after(mark(dve.tensor_tensor(h[:, i, :], h[:, i, :], bout, ALU.add)))
                dve.wait_ge(out_done, i + 1)
                dve.tensor_tensor(h[:, i, :], ps[:, OUT[i % 2][0]:OUT[i % 2][0] + 2, :].rearrange("p b n -> p (b n)"),
                                  h[:, i, :], ALU.add).then_inc(h_ready, 1)

def attention_block(nc, g):
    with ExitStack() as ctx:
        def sb(name, shape, dt=F32):
            return ctx.enter_context(nc.sbuf_tensor("a_" + name, shape, dt))

        def sem(name):
            return g.semaphore(nc, "a_" + name)

        h, ring, ps, ident, vecs = g.h, g.ring, g.ps, g.ident, g.vecs
        gcol = vecs[:, V_MIX + KT:V_MIX + 2 * KT]
        h_dram = nc.dram_tensor("h_dram", [S, D], F32, kind="Internal").ap()
        CH = KT * HALF

        hnT = ring[:, 0:KT * S].rearrange("p (k s) -> p k s", k=KT)
        w_qi, w_q0, w_q1, w_kv = (ring[:, KT * S + n * CH:KT * S + (n + 1) * CH].rearrange("p (k n) -> p k n", k=KT) for n in range(4))
        tok = ring[:, KT * S:KT * S + CH]
        qtok = [tok[:, n * S:(n + 1) * S] for n in range(2)]
        ktok = [tok[:, 2 * S + n * 2 * KVC:2 * S + (n + 1) * 2 * KVC] for n in range(2)]
        probs = [ring[:, n * S:(n + 1) * S] for n in range(3)]
        probsT = [ring[:, (3 + n) * S:(4 + n) * S].rearrange("p (j q) -> p j q", j=T) for n in range(2)]
        otok = ring[:, 5 * S:6 * S]
        oT = ring[:, 6 * S:7 * S].rearrange("p (k q) -> p k q", k=KT)
        resid = [ring[:, 7 * S:8 * S], tok[:, 3 * S:4 * S]]
        w_out = ring[:, KT * S + CH:KT * S + 3 * CH].rearrange("p (k n) -> p k n", k=KT)
        QT = h[:, :, :].rearrange("p t (c q) -> p t c q", c=KT)

        KTd = sb("KTd", [P, NKV, S])
        V = sb("V", [P, T, KVC])
        qiT = sb("qiT", [P, IH // 2, S])
        kiT = V[:, :, :].rearrange("p t c -> p (t c)").rearrange("p (a s) -> p a s", a=2)
        w_ki = sb("w_ki", [P, KT, HD + IH])
        rope = sb("rope", [P, 2, T, ROT // 2])
        kln = sb("kln", [P, 2, HD])
        kiwi = sb("kiwi", [P, T, HD + IH])
        tmp = sb("tmp", [P, 2, H * ROT])
        tmp2 = sb("tmp2", [P, 2, IH * ROT])
        st = sb("st", [P, 4, T])
        max8 = sb("max8", [P, 8])
        offs = [0]
        for i in range(T):
            offs.append(offs[-1] + P * (i + 1))
        score = sb("score", [P, offs[T] - offs[2]])
        bias = sb("bias", [P, offs[T]], BF16)
        mins = sb("mins", [P, H]); rsum = sb("rsum", [P, 2, H]); rinvs = sb("rinvs", [P, H])
        ssum = g.ssum
        rms = sb("rms", [P, T]); rinv = sb("rinv", [P, T])
        KT_of = (KTd, qiT)
        ROWS_OF = (slice(0, HD), slice(HD, 2 * HD))
        hr = KTd[:, 0:2, :]
        junk = sb("junk", [P, D])
        tokI = [bias[:, n * 1024:(n + 1) * 1024].bitcast(F32) for n in range(2)]
        kin = score[:, 0:T * HD].rearrange("p (t d) -> p t d", t=T)
        kin2 = score[:, T * HD:2 * T * HD].rearrange("p (t d) -> p t d", t=T)

        kidup = score[:, 2 * T * HD:4 * T * HD]

        def sc(i):
            return score[:, offs[i] - offs[2]:offs[i + 1] - offs[2]]

        def bi(i):
            return bias[:, offs[i]:offs[i + 1]]

        squared = sem("squared"); meaned = sem("meaned"); rooted = sem("rooted"); step = sem("step")
        hr_ready = sem("hr_ready"); turned = sem("turned"); hnT_ready = sem("hnT_ready")
        spilled = sem("spilled"); padded = sem("padded"); wqi_loaded = sem("wqi_loaded"); wki_loaded = sem("wki_loaded")
        wq_loaded = sem("wq_loaded"); wout_loaded = sem("wout_loaded"); tab_loaded = sem("tab_loaded")
        ki_done = sem("ki_done"); ki_copied = sem("ki_copied"); qi_done = sem("qi_done"); qi_copied = sem("qi_copied"); qi_roped = sem("qi_roped")
        qi_turned = sem("qi_turned"); qiT_ready = sem("qiT_ready")
        ki_var = sem("ki_var"); ki_dev = sem("ki_dev"); ki_ready = sem("ki_ready"); ki_turned = sem("ki_turned")
        kiT_ready = sem("kiT_ready"); dots_done = sem("dots_done"); relu_done = sem("relu_done"); dots_used = sem("dots_used")
        proj_done = sem("proj_done"); q_copied = sem("q_copied"); q_roped = sem("q_roped"); pstep = sem("pstep")
        q_turned = sem("q_turned"); qT_ready = sem("qT_ready")
        qk_done = sem("qk_done"); qk_used = sem("qk_used"); exp_done = sem("exp_done")
        p_turned = sem("p_turned"); t_copied = sem("t_copied"); pv_done = sem("pv_done")
        o_ready = sem("o_ready"); resid_loaded = [sem(f"resid_loaded{n}") for n in range(2)]

        dots = [(i, c, hd) for i in range(2, T) for c in range(0, P * (i + 1), HALF) for hd in range(IH)]
        NB = 6
        KI_LAG = 4
        NS = T * H
        WO_LAG = 3
        SQ_LAG = 5
        qk_order, t_order = [("qk", 0), ("qk", 1)], []
        for s in range(NS + WO_LAG + 1):
            if s + 2 < NS:
                qk_order.append(("qk", s + 2))
            if s < NS:
                t_order.append(("p", s))
            if s >= H and s % H == 1:
                t_order.append(("o", s // H - 1))
            if s >= H and s % H == WO_LAG:
                qk_order.append(("wo", s // H - 1))
        qk_no = {u: n for n, u in enumerate(qk_order)}
        t_no = {u: n for n, u in enumerate(t_order)}

        def keys(s):
            return P * (s // H + 1)

        RPT = TOPK // 8
        rounds = [(i, r) for i in range(2, T) for r in range(RPT)]
        EARLY = 118
        LAST = H * (T - 1) - 4
        RBASE = 64
        BASE = 64

        def rounds_at(s):
            length = [keys(x) + BASE for x in range(LAST)]
            cost = [P * (i + 1) + RBASE for i, _ in rounds[EARLY:]]
            lo, hi = (sum(1 for n in range(len(cost)) if sum(cost[:n]) * sum(length) < sum(cost) * sum(length[:x])) for x in (s, s + 1))
            return rounds[EARLY + lo:EARLY + hi]

        def head(s):
            i, hd = s // H, s % H
            return i, hd // 2, hd % 2, hd // (H // NKV)

        block = ctx.enter_context(nc.Block())

        @block.sync
        def _(sp):
            w = g.dram["attn_w_in"][0].rearrange("(k p) n -> p k n", p=P)
            sp.dma_start(w_ki[:, :, :], w[:, :, QC + 2 * KVC + IH * HD:]).then_inc(wki_loaded, 16)
            sp.dma_start(w_qi, w[:, :, QC + 2 * KVC:QC + 2 * KVC + IH * HD]).then_inc(wqi_loaded, 16)
            sp.dma_start(h_dram.rearrange("(t p) d -> p t d", p=P), h[:, :, :]).then_inc(spilled, 16)
            sp.dma_start(w_q0, w[:, :, 0:HALF]).then_inc(wq_loaded, 16)
            sp.dma_start(w_q1, w[:, :, HALF:2 * HALF]).then_inc(wq_loaded, 16)
            sp.dma_start(w_kv, w[:, :, QC:QC + 2 * KVC]).then_inc(wq_loaded, 16)
            sp.wait_ge(proj_done, T)
            sp.dma_start(w_out, g.dram["attn_w_out"][0].rearrange("(k p) n -> p k n", p=P)).then_inc(wout_loaded, 16)
            sp.wait_ge(qT_ready, 3 * T)
            for i in range(T):
                if i >= 2:
                    sp.wait_ge(qk_used, qk_no[("wo", i - 2)] + 1)
                sp.dma_start(resid[i % 2], h_dram[i * P:(i + 1) * P, :]).then_inc(resid_loaded[i % 2], 16)

        @block.gpsimd
        def _(pool):
            for a in range(2):
                pool.memset(kiT[ROWS_OF[1 - a], a, :], 0.0).then_inc(padded, 1)
                pool.wait_ge(padded, a + 1)
            pool.wait_ge(turned, T)
            pool.memset(KTd[ROWS_OF[1], :, :], 0.0).then_inc(padded, 1)
            pool.wait_ge(dots_done, len(dots))
            pool.wait_ge(padded, 3)
            pool.memset(qiT[ROWS_OF[0], :, :], 0.0).then_inc(padded, 1)
            pool.wait_ge(padded, 4)
            pool.wait_ge(tab_loaded, 64)
            count = [0]

            def chain(ins):
                count[0] += 1
                ins.then_inc(pstep, 1)
                pool.wait_ge(pstep, count[0])

            def rotate(buf, n, i, done):
                x = buf.rearrange("p (n d) -> p n d", d=HD)[:, :, 0:ROT].rearrange("p n (a c) -> p n a c", a=2)
                half = ROT // 2
                shape = [P, n, half]
                c, s = (rope[:, q, i, :].unsqueeze(1).to_broadcast(shape) for q in range(2))
                t = [tmp[:, q, 0:n * ROT].rearrange("p (n a c) -> p n a c", n=n, a=2) for q in range(2)]
                for a in range(2):
                    pool.tensor_tensor(t[0][:, :, a, :], x[:, :, a, :], c, ALU.mult)
                    last = pool.tensor_tensor(t[1][:, :, a, :], x[:, :, a, :], s, ALU.mult)
                chain(last)
                pool.tensor_tensor(x[:, :, 0, :], t[0][:, :, 0, :], t[1][:, :, 1, :], ALU.subtract)
                last = pool.tensor_tensor(x[:, :, 1, :], t[0][:, :, 1, :], t[1][:, :, 0, :], ALU.add)
                if done is None:
                    chain(last)
                else:
                    last.then_inc(done, 1)

            for i in range(T):
                pool.wait_ge(q_copied, i + 1)
                if i >= 1:
                    pool.wait_ge(q_roped, i)
                rotate(qtok[i % 2], H, i, None)
                rotate(ktok[i % 2], 2 * NKV, i, q_roped)

        @block.scalar
        def _(act):
            for q in range(2):
                act.dma_start(rope[:, q, :, :], g.dram["rope"][q].rearrange("(t p) c -> p t c", p=P)).then_inc(tab_loaded, 16)
            act.dma_start(kln[:, 0, :], g.dram["idx_k_ln_g"][0].partition_broadcast(P)).then_inc(tab_loaded, 16)
            act.dma_start(kln[:, 1, :], g.dram["idx_k_ln_b"][0].partition_broadcast(P)).then_inc(tab_loaded, 16)

            act.wait_ge(meaned, 1)
            act.activation(rms[:, :], ssum[:, :], ACT.Sqrt).then_inc(rooted, 1)

            def copy_qiT(i):
                act.wait_ge(qi_turned, i + 1)
                act.activation(qiT[:, :, i * P:(i + 1) * P], ps[:, 4 + i % 2, :].rearrange("p (c q) -> p c q", q=P), ACT.Copy).then_inc(qiT_ready, 1)

            act.wait_ge(ki_done, T)
            for b in range(2):
                act.activation(kiwi[:, b * T // 2:(b + 1) * T // 2, :],
                               ps[:, 6 + b, 0:T // 2 * (HD + IH)].rearrange("p (t n) -> p t n", n=HD + IH), ACT.Copy).then_inc(ki_copied, 1)
            for i in range(T):
                act.wait_ge(qi_done, i + 1)
                if i >= 2:
                    act.wait_ge(qi_turned, i - 1)
                act.activation(tokI[i % 2], ps[:, i % 2, :], ACT.Copy).then_inc(qi_copied, 1)
                if i == 0:
                    act.wait_ge(ki_var, 1)
                    act.activation(st[:, 2, :], st[:, 1, :], ACT.Sqrt).then_inc(ki_dev, 1)
                if i >= 1:
                    copy_qiT(i - 1)
                if i == KI_LAG:
                    act.wait_ge(ki_turned, 1)
                    for a in range(2):
                        act.activation(kiT[ROWS_OF[a], a, :], ps[ROWS_OF[a], 6:8, :].rearrange("p b n -> p (b n)"), ACT.Copy).then_inc(kiT_ready, 1)
            copy_qiT(T - 1)
            for n, (i, c, hd) in enumerate(dots):
                w = min(HALF, P * (i + 1) - c)
                act.wait_ge(dots_done, n + 1)
                act.activation(ps[:, n % NB, 0:w], ps[:, n % NB, 0:w], ACT.Relu).then_inc(relu_done, 1)

            act.wait_ge(dots_used, len(dots))
            act.wait_ge(spilled, 16)
            act.wait_ge(hr_ready, T)

            def copy_qk(i, parts):
                for part in parts:
                    act.wait_ge(q_turned, 3 * i + part + 1)
                    src = ps[:, 6 + part % 2, :].rearrange("p (c q) -> p c q", q=P)
                    if part < 2:
                        act.activation(QT[:, i, 4 * part:4 * part + 4, :], src, ACT.Copy).then_inc(qT_ready, 1)
                    else:
                        act.activation(KT_of[0][ROWS_OF[0], :, i * P:(i + 1) * P], src[ROWS_OF[0]], ACT.Copy)
                        act.activation(KT_of[1][ROWS_OF[1], :, i * P:(i + 1) * P], src[ROWS_OF[1]], ACT.Copy).then_inc(qT_ready, 1)

            for i in range(T):
                if i >= 1:
                    copy_qk(i - 1, (0, 1))
                act.wait_ge(proj_done, i + 1)
                if i >= 2:
                    act.wait_ge(q_turned, 3 * (i - 1))
                b = 3 * (i % 2)
                act.activation(qtok[i % 2], ps[:, b:b + 2, :].rearrange("p b n -> p (b n)"), ACT.Copy)
                act.activation(ktok[i % 2].rearrange("p (n a d) -> p n a d", a=2, d=HD),
                               ps[:, b + 2, 0:KVC].rearrange("p (n d) -> p n d", d=HD).unsqueeze(2).to_broadcast([P, NKV, 2, HD]), ACT.Copy)
                act.activation(V[:, i, :], ps[:, b + 2, KVC:2 * KVC], ACT.Copy).then_inc(q_copied, 1)
                if i >= 1:
                    copy_qk(i - 1, (2,))
            copy_qk(T - 1, range(3))

            def exps(s):
                act.wait_ge(qk_used, qk_no[("qk", s)] + 1)
                buf = probs[s % 3][:, 0:keys(s)]
                act.activation(buf, buf, ACT.Exp, scale=-1.0, bias=mins[:, s % H:s % H + 1],
                               accum_out=rsum[:, (s // H) % 2, s % H:s % H + 1]).then_inc(exp_done, 1)

            def copy_turned(u, dst):
                act.wait_ge(p_turned, t_no[u] + 1)
                act.activation(dst, ps[:, 4:6, :].rearrange("p b (j q) -> p (b j) q", q=P)[:, 0:dst.shape[1], :], ACT.Copy).then_inc(t_copied, 1)

            exps(0)
            exps(1)
            for s in range(NS + SQ_LAG + 1):
                if s < NS:
                    if s >= 2:
                        act.wait_ge(pv_done, s - 1)
                    copy_turned(("p", s), probsT[s % 2][:, 0:keys(s) // P, :])
                if ("o", s // H - 1) in t_no and s % H == 1 and s >= H:
                    copy_turned(("o", s // H - 1), oT)
                if s + 2 < NS:
                    exps(s + 2)
                if s >= H and s % H == SQ_LAG:
                    i = s // H - 1
                    act.wait_ge(qk_used, qk_no[("wo", i)] + 1)
                    if i >= 1:
                        act.wait_ge(squared, i)
                    act.activation(junk[:, :], h[:, i, :], ACT.Square, accum_out=ssum[:, i:i + 1]).then_inc(squared, 1)

        @block.tensor
        def _(pe):
            def keys_of(i):
                pe.wait_ge(hnT_ready, i + 1)
                if i == 0:
                    pe.wait_ge(wki_loaded, 16)
                n = HD + IH
                for k in range(KT):
                    last = pe.matmul(ps[:, 6 + i // 4, (i % 4) * n:(i % 4 + 1) * n], hnT[:, k, i * P:(i + 1) * P], w_ki[:, k, :],
                                     start=(k == 0), stop=(k == KT - 1))
                last.then_inc(ki_done, 1)

            for i in range(T):
                pe.wait_ge(hr_ready, i + 1)
                if i >= 2:
                    pe.wait_ge(hnT_ready, i - 1)
                tps = ps[:, 2 * (i % 2):2 * (i % 2) + 2, :].rearrange("p b (k c) -> p (b k) c", c=P)
                for k in range(KT):
                    last = pe.transpose(tps[:, k, :], hr[:, i % 2, k * P:(k + 1) * P], ident[:, :])
                last.then_inc(turned, 1)
                if i >= 2:
                    keys_of(i - 2)

            def turn_qi(i):
                pe.wait_ge(qi_roped, i + 1)
                if i >= 2:
                    pe.wait_ge(qiT_ready, i - 1)
                for c in range(4):
                    last = pe.transpose(ps[:, 4 + i % 2, c * P:(c + 1) * P], tokI[i % 2][:, c * P:(c + 1) * P], ident[:, :])
                last.then_inc(qi_turned, 1)

            def project(bank, w, i, n):
                for k in range(KT):
                    last = pe.matmul(ps[:, bank, 0:n], hnT[:, k, i * P:(i + 1) * P], w[:, k, 0:n], start=(k == 0), stop=(k == KT - 1))
                return last

            keys_of(T - 2)
            keys_of(T - 1)
            pe.wait_ge(wqi_loaded, 16)
            for i in range(T):
                if i >= 2:
                    pe.wait_ge(qi_copied, i - 1)
                project(i % 2, w_qi, i, HALF).then_inc(qi_done, 1)
                if i >= 1:
                    turn_qi(i - 1)
                if i == KI_LAG:
                    pe.wait_ge(ki_ready, 1)
                    for t in range(T):
                        last = pe.transpose(ps[:, 6 + t // 4, (t % 4) * P:(t % 4 + 1) * P], kidup[:, t * P:(t + 1) * P], ident[:, :])
                    last.then_inc(ki_turned, 1)
            turn_qi(T - 1)
            pe.wait_ge(kiT_ready, 2)
            pe.wait_ge(qiT_ready, T)
            pe.wait_ge(padded, 2)
            for n, (i, c, hd) in enumerate(dots):
                w = min(HALF, P * (i + 1) - c)
                if n >= NB:
                    pe.wait_ge(dots_used, n - NB + 1)
                pe.matmul(ps[:, n % NB, 0:w], qiT[:, hd // 2, i * P:(i + 1) * P], kiT[:, hd % 2, c:c + w],
                          start=True, stop=True).then_inc(dots_done, 1)

            def turn_qk(i, part):
                pe.wait_ge(q_roped, i + 1)
                if i >= 1 or part == 2:
                    pe.wait_ge(qT_ready, 3 * i + (0, -1, 1)[part])
                for c in range(4):
                    src = (qtok[i % 2][:, (4 * part + c) * P:(4 * part + c + 1) * P] if part < 2 else
                           ktok[i % 2][:, c * P:(c + 1) * P])
                    last = pe.transpose(ps[:, 6 + part % 2, c * P:(c + 1) * P], src, ident[:, :])
                last.then_inc(q_turned, 1)

            pe.wait_ge(dots_used, len(dots))
            pe.wait_ge(wq_loaded, 48)
            for i in range(T):
                if i >= 2:
                    pe.wait_ge(q_copied, i - 1)
                b = 3 * (i % 2)
                project(b, w_q0, i, HALF)
                project(b + 1, w_q1, i, HALF)
                if i >= 1:
                    turn_qk(i - 1, 0)
                    turn_qk(i - 1, 1)
                project(b + 2, w_kv, i, HALF).then_inc(proj_done, 1)
                if i >= 1:
                    turn_qk(i - 1, 2)
            for part in range(3):
                turn_qk(T - 1, part)
            pe.wait_ge(qT_ready, 3 * T)
            pe.wait_ge(padded, 4)

            def qk(s):
                i, c, a, n = head(s)
                no = qk_no[("qk", s)]
                if no >= 2:
                    pe.wait_ge(qk_used, no - 1)
                for k0 in range(0, keys(s), HALF):
                    w = min(HALF, keys(s) - k0)
                    last = pe.matmul(ps[:, 2 * (no % 2) + k0 // HALF, 0:w], QT[:, i, c, :], KT_of[a][:, n, k0:k0 + w],
                                     start=True, stop=True)
                last.then_inc(qk_done, 1)

            def turn(u, src, n):
                no = t_no[u]
                if no >= 1:
                    pe.wait_ge(t_copied, no)
                for j in range(n):
                    last = pe.transpose(ps[:, 4 + j // 4, (j % 4) * P:(j % 4 + 1) * P], src[:, j * P:(j + 1) * P], ident[:, :])
                last.then_inc(p_turned, 1)

            def pv(s):
                i, _, _, n = head(s)
                pe.wait_ge(t_copied, t_no[("p", s)] + 1)
                if s % H == 0 and i >= 1:
                    pe.wait_ge(o_ready, i)
                hd = s % H
                for j in range(i + 1):
                    last = pe.matmul(ps[:, 6 + hd // 8, (hd % 8) * HD:(hd % 8 + 1) * HD], probsT[s % 2][:, j, :],
                                     V[:, j, n * HD:(n + 1) * HD], start=(j == 0), stop=(j == i))
                last.then_inc(pv_done, 1)

            def output(i):
                no = qk_no[("wo", i)]
                pe.wait_ge(qk_used, no - 1)
                pe.wait_ge(t_copied, t_no[("o", i)] + 1)
                for b in range(2):
                    for k in range(KT):
                        last = pe.matmul(ps[:, 2 * (no % 2) + b, :], oT[:, k, :], w_out[:, k, b * HALF:(b + 1) * HALF],
                                         start=(k == 0), stop=(k == KT - 1))
                last.then_inc(qk_done, 1)

            qk(0)
            qk(1)
            for s in range(NS + WO_LAG + 1):
                if s + 2 < NS:
                    qk(s + 2)
                if s < NS:
                    pe.wait_ge(exp_done, s + 1)
                    turn(("p", s), probs[s % 3], keys(s) // P)
                if 1 <= s <= NS:
                    pv(s - 1)
                if s >= H and s % H == 1:
                    pe.wait_ge(o_ready, s // H)
                    turn(("o", s // H - 1), otok, KT)
                if s >= H and s % H == WO_LAG:
                    if s // H == 1:
                        pe.wait_ge(wout_loaded, 16)
                    output(s // H - 1)

        @block.vector
        def _(dve):
            count = [0]

            def mark(ins):
                count[0] += 1
                ins.then_inc(step, 1)
                return count[0]

            def chain(ins):
                dve.wait_ge(step, mark(ins))

            def evacuate(i):
                dve.wait_ge(turned, i + 1)
                tps = ps[:, 2 * (i % 2):2 * (i % 2) + 2, :].rearrange("p b (k c) -> p (b k) c", c=P)
                dve.tensor_tensor(hnT[:, :, i * P:(i + 1) * P], tps, gcol.unsqueeze(2).to_broadcast([P, KT, P]),
                                  ALU.mult).then_inc(hnT_ready, 1)

            dve.tensor_scalar(ssum[:, :], ssum[:, :], 1.0 / D, EPS, ALU.mult, ALU.add).then_inc(meaned, 1)
            dve.wait_ge(rooted, 1)
            chain(dve.reciprocal(rinv[:, :], rms[:, :]))
            for i in range(T):
                if i >= 2:
                    evacuate(i - 2)
                dve.tensor_scalar(hr[:, i % 2, :], h[:, i, :], rinv[:, i:i + 1], None, ALU.mult).then_inc(hr_ready, 1)
            evacuate(T - 2)
            evacuate(T - 1)
            dve.wait_ge(tab_loaded, 64)

            def rotate(x3, cos, sin, n, done):
                x = x3[:, :, 0:ROT].rearrange("p n (a c) -> p n a c", a=2)
                t = [tmp2[:, q, 0:n * ROT].rearrange("p (n a c) -> p n a c", n=n, a=2) for q in range(2)]
                for a in range(2):
                    dve.tensor_tensor(t[0][:, :, a, :], x[:, :, a, :], cos, ALU.mult)
                    last = dve.tensor_tensor(t[1][:, :, a, :], x[:, :, a, :], sin, ALU.mult)
                chain(last)
                dve.tensor_tensor(x[:, :, 0, :], t[0][:, :, 0, :], t[1][:, :, 1, :], ALU.subtract)
                last = dve.tensor_tensor(x[:, :, 1, :], t[0][:, :, 1, :], t[1][:, :, 0, :], ALU.add)
                if done is None:
                    chain(last)
                else:
                    last.then_inc(done, 1)

            def bct(v, n):
                return v.unsqueeze(2).to_broadcast([P, T, n])
            ki = kiwi[:, :, 0:HD]
            dve.wait_ge(ki_copied, 2)
            chain(dve.tensor_reduce(st[:, 0, :], ki, AX.X, ALU.add))
            chain(dve.tensor_scalar(st[:, 0, :], st[:, 0, :], 1.0 / HD, None, ALU.mult))
            chain(dve.tensor_tensor(kin, ki, bct(st[:, 0, :], HD), ALU.subtract))
            chain(dve.tensor_tensor(kin2, kin, kin, ALU.mult))
            chain(dve.tensor_reduce(st[:, 1, :], kin2, AX.X, ALU.add))
            dve.tensor_scalar(st[:, 1, :], st[:, 1, :], 1.0 / HD, EPS, ALU.mult, ALU.add).then_inc(ki_var, 1)
            dve.wait_ge(ki_dev, 1)
            chain(dve.reciprocal(st[:, 3, :], st[:, 2, :]))
            chain(dve.tensor_tensor(kin, kin, bct(st[:, 3, :], HD), ALU.mult))
            chain(dve.tensor_tensor(kin, kin, kln[:, 0, :].unsqueeze(1).to_broadcast([P, T, HD]), ALU.mult))
            chain(dve.tensor_tensor(kin2, kin, kln[:, 1, :].unsqueeze(1).to_broadcast([P, T, HD]), ALU.add))
            rotate(kin2, rope[:, 0, :, :], rope[:, 1, :, :], T, None)
            dve.tensor_copy(kidup.rearrange("p (t a d) -> p t a d", a=2, d=HD),
                            kin2.unsqueeze(2).to_broadcast([P, T, 2, HD])).then_inc(ki_ready, 1)
            wi = kiwi[:, :, HD:HD + IH]
            chain(dve.tensor_scalar(wi, wi, float(IH) ** -0.5 * float(HD) ** -0.5, None, ALU.mult))

            for i in range(T):
                dve.wait_ge(qi_copied, i + 1)
                if i >= 1:
                    dve.wait_ge(qi_roped, i)
                cos, sin = (rope[:, q, i, :].unsqueeze(1).to_broadcast([P, IH, ROT // 2]) for q in range(2))
                rotate(tokI[i % 2].rearrange("p (n d) -> p n d", d=HD), cos, sin, IH, qi_roped)

            def edge(ap, i, value):
                n = P * (i + 1)
                return dve.memset(ap[0:CHUNK, n - CHUNK:n], value)

            dve.wait_ge(ki_turned, 1)
            last = {}
            for n, (i, c, hd) in enumerate(dots):
                w = min(HALF, P * (i + 1) - c)
                dst = sc(i)[:, c:c + w]
                dve.wait_ge(relu_done, n + 1)
                if hd == 0:
                    dve.tensor_scalar(dst, ps[:, n % NB, 0:w], kiwi[:, i, HD:HD + 1], None, ALU.mult).then_inc(dots_used, 1)
                else:
                    dve.wait_ge(dots_used, n)
                    dve.scalar_tensor_tensor(dst, ps[:, n % NB, 0:w], kiwi[:, i, HD + hd:HD + hd + 1], dst, ALU.mult, ALU.add).then_inc(dots_used, 1)
            dve.wait_ge(dots_used, len(dots))
            dve.wait_ge(qi_turned, T)
            for i in range(2):
                chain(dve.memset(bi(i), 0.0))
                chain(edge(bi(i), i, -NEG))

            def search(i, r):
                s = sc(i)
                if r == 0:
                    chain(edge(s, i, INADMISSIBLE))
                chain(dve.max(max8[:, :], s))
                chain(dve.match_replace(s, max8[:, :], s, TAKEN))
                if r == RPT - 1:
                    chain(dve.tensor_scalar(bi(i), s, INADMISSIBLE * 2, -NEG, ALU.is_gt, ALU.mult))

            for i, r in rounds[:EARLY]:
                search(i, r)

            def masked(s):
                no = qk_no[("qk", s)]
                dve.wait_ge(qk_done, no + 1)
                if s >= 3:
                    dve.wait_ge(p_turned, t_no[("p", s - 3)] + 1)
                if s >= H:
                    dve.wait_ge(exp_done, s - H + 1)
                n = keys(s)
                b = 2 * (no % 2)
                dve.tensor_tensor_reduce(probs[s % 3][:, 0:n], ps[:, b:b + 2, :].rearrange("p b n -> p (b n)")[:, 0:n], bi(s // H),
                                         -float(HD) ** -0.5, 3e38, ALU.add, ALU.min, mins[:, s % H:s % H + 1]).then_inc(qk_used, 1)

            def output(i):
                no = qk_no[("wo", i)]
                dve.wait_ge(qk_done, no + 1)
                dve.wait_ge(resid_loaded[i % 2], 16 * (i // 2 + 1))
                b = 2 * (no % 2)
                dve.tensor_tensor(h[:, i, :], ps[:, b:b + 2, :].rearrange("p b n -> p (b n)"), resid[i % 2], ALU.add).then_inc(qk_used, 1)

            dve.wait_ge(qT_ready, 3 * T)
            masked(0)
            masked(1)
            for s in range(NS + WO_LAG + 1):
                if s >= H and s % H == 0:
                    i = s // H - 1
                    dve.wait_ge(pv_done, s)
                    dve.wait_ge(exp_done, s)
                    chain(dve.reciprocal(rinvs[:, :], rsum[:, i % 2, :]))
                    if i >= 1:
                        dve.wait_ge(p_turned, t_no[("o", i - 1)] + 1)
                    dve.tensor_tensor(otok.rearrange("p (n d) -> p n d", d=HD), ps[:, 6:8, :].rearrange("p b (n d) -> p (b n) d", d=HD),
                                      rinvs[:, :].unsqueeze(2).to_broadcast([P, H, HD]), ALU.mult).then_inc(o_ready, 1)
                if s + 2 < NS:
                    masked(s + 2)
                if s >= H and s % H == WO_LAG:
                    output(s // H - 1)
                for i, r in rounds_at(s):
                    search(i, r)

def moe_block(nc, g, layer, after):
    with ExitStack() as ctx:
        pre = f"m{layer}_"

        def sb(name, shape, dt=F32):
            return ctx.enter_context(nc.sbuf_tensor(pre + name, shape, dt))

        def sem(name):
            return g.semaphore(nc, pre + name)

        h, ring, ps, ident = g.h, g.ring, g.ps, g.ident
        hr_dram = nc.dram_tensor(pre + "hr_dram", [S, D], F32, kind="Internal").ap()
        y_dram = g.y_dram

        hw = sb("hw", [P, AHEAD, D], F32R)
        spare = nc.alloc_sbuf_tensor_at(pre + "spare", [P, (AHEAD - EARLY) * D], F32, offset=nc.sbuf_base - 4 * (AHEAD - EARLY) * D)
        xhl = sb("xhl", [P, 2, 2, KT, P], F32R)
        hhl = sb("hhl", [P, 2, ET, P], F32R)
        hnT = nc.alloc_sbuf_tensor_at(pre + "hnT", [P, 2, KT, P], F32, offset=nc.sbuf_base - 4 * (2 * ET * P + 2 * KT * P))
        rows = nc.alloc_sbuf_tensor_at(pre + "rows", [P, ROWBUFS, 2, D], F32, offset=nc.sbuf_base - 4 * (2 * ET * P + 4 * KT * P + AHEAD * D))
        ring_low = [nc.alloc_sbuf_tensor_at(f"{pre}ring_low{u}", [P, SLOT], F32R, offset=g.ring_at + 4 * u * SLOT) for u in range(2)]
        hr = sb("hr", [P, 2, D])
        xg = sb("xg", [P, 2, D])
        y = hr
        act_tile = sb("act_tile", [P, 2, DE])
        sg, hb = act_tile[:, 0, :], act_tile[:, 1, :]
        sq = act_tile[:, :, :].rearrange("p a n -> p (a n)")
        gains = sb("gains", [P, D])
        ssum = g.ssum
        rms = sb("rms", [P, T]); rinv = sb("rinv", [P, T])
        tokid = sb("tokid", [P, T])
        ones_b = sb("ones_b", [P, P], BF16)
        tri_b = sb("tri_b", [P, P], BF16)
        ohb = sb("ohb", [P, T, NE], BF16)
        wts = sb("wts", [P, 2, T])
        novi = sb("novi", [P, NE], I32); sloti = sb("sloti", [P, 2, T], I32)
        blki = sb("blki", [P, 2, T], I32); loi = sb("loi", [P, 2, T], I32)
        slotu = sb("slotu", [P, 2 * T], U32)
        toku = sb("toku", [P, NBLK], U32)
        eidi = sb("eidi", [P, NOVER + 1], I32)

        place = [0]

        def early(a, b, c):
            at = place[0]
            place[0] += a * b * c
            return spare[:, at:place[0]].rearrange("p (a b c) -> p a b c", a=a, b=b)

        lg = early(1, T, NR)[:, 0]; em = early(1, T, NE)[:, 0]; ea = early(1, T, NE)[:, 0]
        slotm = early(1, T, NE)[:, 0]; oh = early(2, T, NE)
        eidc = early(1, NOVER, NE)[:, 0]
        wr = early(1, KT, NR)[:, 0]
        rbias, pri, cap1, zeros, novf, obend, dlt = (early(1, 1, n)[:, 0, 0] for n in (NR, NE, NE, NE, NE, NE, NE))
        iota = early(1, 1, P)[:, 0, 0]; eid = early(1, 1, NOVER)[:, 0, 0]
        ga = early(1, T, NG)[:, 0]; goh = early(1, T, NG)[:, 0]; small = early(1, 16, T)[:, 0]
        slot = early(1, 2, T)[:, 0]; blk = early(1, 2, T)[:, 0]; lo = early(1, 2, T)[:, 0]
        Bm = xg[:, :, :].rearrange("p a n -> p (a n)")[:, 0:2 * T * NBLK].rearrange("p (a n) -> p a n", n=NBLK)
        Am = hr[:, :, :].rearrange("p a (b c) -> p (a b) c", c=P)

        meaned = sem("meaned"); rooted = sem("rooted"); step = sem("step")
        hr_ready = sem("hr_ready"); hr_stored = [sem(f"hr_stored{u}") for u in range(2)]
        turned = sem("turned"); hnT_ready = sem("hnT_ready"); routed = sem("routed")
        small_loaded = sem("small_loaded"); consts = sem("consts")
        ebias = sem("ebias"); expd = sem("expd"); ohb_ready = sem("ohb_ready"); ranked = sem("ranked")
        ab_ready = sem("ab_ready"); listed = sem("listed"); lists_ready = sem("lists_ready")
        xg_loaded = [sem(f"xg_loaded{u}") for u in range(2)]
        x_turned = sem("x_turned"); x_high = sem("x_high"); x_low = sem("x_low")
        used = sem("used"); high = sem("high"); low = sem("low"); silu_done = sem("silu_done"); hb_ready = sem("hb_ready")
        h_turned = sem("h_turned"); h_high = sem("h_high"); h_low = sem("h_low")
        y_ready = sem("y_ready"); gains_loaded = sem("gains_loaded"); y_stored = [sem(f"y_stored{u}") for u in range(2)]
        loaded = [[sem(f"{name}_loaded{u}") for u in range(2)] for name in ("gate", "up", "down")]
        o_loaded = sem("o_loaded"); o_gathered = sem("o_gathered");
        r_loaded = [sem(f"r_loaded{u}") for u in range(ROWBUFS)]; combined = sem("combined")
        f_sq = sem("f_sq"); f_mean = sem("f_mean"); f_root = sem("f_root"); f_out = sem("f_out"); f_stored = [sem(f"f_stored{u}") for u in range(2)]
        if after:
            final_loaded = sem("final_loaded")

        GATE, UP, DOWN, HT = 2, 3, (4, 5), 6
        ROUTE, RANK = 7, 6

        def turn_ps(pair=0):
            return ps[:, 2 * pair:2 * pair + 2, :].rearrange("p b (k c) -> p (b k) c", c=P)

        def gu_piece(e):
            return NPIECE * e - ET

        def down_piece(e):
            return NPIECE * (e + 1) + GU_PIECES - ET

        def raw(u, q):
            return ring[:, u * SLOT + q * D:u * SLOT + (q + 1) * D]

        def lowp(u, q):
            return ring_low[u][:, q * D:(q + 1) * D]

        def over_loop(eng):
            return eng.value_load(eidi[0:1, NOVER:NOVER + 1], min_val=0, max_val=NOVER)

        block = ctx.enter_context(nc.Block())

        @block.sync
        def _(sp):
            for i in range(T):
                sp.wait_ge(hr_ready, i + 1)
                sp.dma_start(hr_dram[i * P:(i + 1) * P, :], hr[:, i % 2, :]).then_inc(hr_stored[i % 2], 16)

            def load(e, u, matrix, arrived):
                name = ("moe_w_gate", "moe_w_up", "moe_w_down")[matrix]
                sp.dma_start(expert_weights(ring, u)[matrix],
                             g.dram[name][layer, bass.ds(e, 1)].rearrange("e (k p) n -> p (e k) n", p=P)).then_inc(arrived, 16)

            for u in range(2):
                for matrix in range(3):
                    load(u, u, matrix, loaded[matrix][u])

            def store_y(e, u):
                sp.wait_ge(y_ready, e + 1)
                sp.dma_start(y_dram[bass.ds(e * P, P), :], y[:, u, :]).then_inc(y_stored[u], 16)

            def after_products(e, u):
                sp.wait_ge(used, gu_piece(e) + GATE_PIECES)
                load(e + 2, u, 0, loaded[0][u])
                sp.wait_ge(used, gu_piece(e) + GU_PIECES)
                load(e + 2, u, 1, loaded[1][u])
                sp.wait_ge(used, down_piece(e - 1) + ET)
                load(e + 1, 1 - u, 2, loaded[2][1 - u])
                store_y(e - 1, 1 - u)

            sp.wait_ge(used, GATE_PIECES)
            load(2, 0, 0, loaded[0][0])
            sp.wait_ge(used, GU_PIECES)
            load(2, 0, 1, loaded[1][0])
            with sp.Fori(0, NE // 2 - 2) as i:
                after_products(2 * i + 1, 1)
                after_products(2 * i + 2, 0)
            after_products(NE - 3, 1)
            sp.wait_ge(used, down_piece(NE - 3) + ET)
            load(NE - 1, 1, 2, loaded[2][1])
            for e in range(NE - 3, NE):
                store_y(e, e % 2)
            n_over = over_loop(sp)
            with sp.If(n_over > 0):
                with sp.Fori(0, n_over) as j:
                    e = sp.value_load(eidi[0:1, bass.ds(j, 1)], min_val=0, max_val=NE - 1)
                    sp.wait_ge(used, NPIECE * (NE + j))
                    sp.wait_ge(y_stored[0], 16 * (NE // 2) + 16 * j)
                    for matrix in range(3):
                        load(e, 0, matrix, o_loaded)
                    sp.wait_ge(y_ready, NE + 1 + j)
                    sp.dma_start(y_dram[bass.ds((NE + j) * P, P), :], y[:, 0, :]).then_inc(y_stored[0], 16)
            if after:
                for i in range(T):
                    sp.wait_ge(f_out, i + 1)
                    sp.dma_start(g.dram["out"][0, i * P:(i + 1) * P, :], hnT[:, i % 2, :, :].rearrange("p k c -> p (k c)")).then_inc(f_stored[i % 2], 16)
                for u in range(2):
                    sp.wait_ge(f_stored[u], 16 * T // 2)

        @block.gpsimd
        def _(pool):
            pool.memset(ones_b[:, :], 1.0).then_inc(consts, 1)
            pool.memset(tri_b[:, :], 1.0).then_inc(consts, 1)
            pool.memset(zeros[:, :], 0.0).then_inc(consts, 1)
            pool.iota(pri[:, :], pattern=[[-1, NE]], base=NE, channel_multiplier=0, allow_small_or_imprecise_dtypes=True).then_inc(consts, 1)
            pool.iota(iota[:, :], pattern=[[1, P]], base=0, channel_multiplier=0, allow_small_or_imprecise_dtypes=True).then_inc(consts, 1)
            pool.iota(tokid[:, :], pattern=[[P, T]], base=0, channel_multiplier=1, allow_small_or_imprecise_dtypes=True).then_inc(consts, 1)
            pool.iota(cap1[:, :], pattern=[[P, NE]], base=0, channel_multiplier=0, allow_small_or_imprecise_dtypes=True).then_inc(consts, 1)
            pool.wait_ge(consts, 7)
            pool.affine_select(out=tri_b[:, :], in_=tri_b[:, :], compare_op=ALU.is_gt, fill=0.0, base=0,
                               pattern=[[1, P]], channel_multiplier=-1).then_inc(consts, 1)
            pool.wait_ge(lists_ready, 1)
            for u in range(2):
                pool.wait_ge(hr_stored[u], 16 * T // 2)

            def gather(e, u, arrived):
                pool.indirect_dma_start(xg[:, u, :], None, hr_dram[:, :],
                                        bass.IndirectOffsetOnAxis(ap=toku[:, e:e + 1], axis=0)).then_inc(arrived, 16)

            for e in range(NE):
                if e >= 2:
                    pool.wait_ge(x_turned, e - 1)
                gather(e, e % 2, xg_loaded[e % 2])
            n_over = over_loop(pool)
            for j in range(NOVER):
                with pool.If(n_over > j):
                    pool.wait_ge(x_turned, NE + j)
                    gather(NE + j, 0, o_gathered)
            for u in range(2):
                pool.wait_ge(y_stored[u], 16 * NE // 2)
            with pool.If(n_over > 0):
                pool.wait_ge(y_stored[0], n_over * 16 + 16 * (NE // 2))
            for i in range(T):
                if i >= ROWBUFS:
                    pool.wait_ge(combined, 2 * (i - ROWBUFS + 1))
                for a in range(2):
                    pool.indirect_dma_start(rows[:, i % ROWBUFS, a, :], None, y_dram[:, :],
                                            bass.IndirectOffsetOnAxis(ap=slotu[:, a * T + i:a * T + i + 1], axis=0)).then_inc(r_loaded[i % ROWBUFS], 16)

        @block.scalar
        def _(act):
            act.dma_start(gains[:, :], g.dram["ffn_norm_g"][layer].partition_broadcast(P)).then_inc(gains_loaded, 16)
            act.dma_start(wr[:, :, 0:NG], g.dram["moe_w_group"][layer].rearrange("(k p) n -> p k n", p=P)).then_inc(small_loaded, 16)
            act.dma_start(wr[:, :, NG:NR], g.dram["moe_w_router"][layer].rearrange("(k p) n -> p k n", p=P)).then_inc(small_loaded, 16)
            act.dma_start(rbias[:, 0:NG], g.dram["moe_b_group"][layer].partition_broadcast(P)).then_inc(small_loaded, 16)
            act.dma_start(rbias[:, NG:NR], g.dram["moe_b_router"][layer].partition_broadcast(P)).then_inc(small_loaded, 16)

            def square(i):
                if i >= 1:
                    act.wait_ge(squared, i)
                act.activation(sq[:, :], h[:, i, :], ACT.Square, accum_out=ssum[:, i:i + 1]).then_inc(squared, 1)

            act.wait_ge(meaned, 1)
            act.activation(rms[:, :], ssum[:, :], ACT.Sqrt).then_inc(rooted, 1)
            if after:
                act.wait_ge(hr_ready, T)
                act.dma_start(gains[:, :], g.dram["final_norm_g"].partition_broadcast(P)).then_inc(final_loaded, 16)
            act.wait_ge(ebias, 1)
            act.activation(ga[:, :, :], ga[:, :, :], ACT.Exp).then_inc(expd, 1)
            act.wait_ge(ebias, 2)
            act.activation(small[:, 5, :], small[:, 4, :], ACT.Exp).then_inc(expd, 1)

            def split_high(n, at, src):
                if not isinstance(n, int) or n >= AHEAD:
                    act.wait_ge(used, n - AHEAD + 1)
                act.activation(hw[:, at % AHEAD, :], src, ACT.Copy).then_inc(high, 1)

            def gate_high(e, u, at, count):
                act.wait_ge(loaded[0][u], 16 * count)
                for q in range(GATE_PIECES):
                    split_high(gu_piece(e) + q, at + q, raw(u, q))

            def up_high(e, u, at, count):
                act.wait_ge(loaded[1][u], 16 * count)
                for q in range(GATE_PIECES, GU_PIECES):
                    split_high(gu_piece(e) + q, at + q, raw(u, q))

            def down_high(first, u, at, count):
                act.wait_ge(loaded[2][u], 16 * count)
                for q in range(ET):
                    split_high(first + q, at + q, raw(u, GU_PIECES + q))

            def x_to_high(e, u):
                act.wait_ge(x_turned, e + 1)
                act.activation(xhl[:, u, 0, :, :], turn_ps(), ACT.Copy).then_inc(x_high, 1)

            def silu(gate_done):
                act.wait_ge(used, gate_done)
                act.activation(sg, ps[:, GATE, :], ACT.Silu).then_inc(silu_done, 1)

            def h_to_high(e):
                act.wait_ge(h_turned, e + 1)
                act.activation(hhl[:, 0, :, :], ps[:, HT, :].rearrange("p (k c) -> p k c", c=P), ACT.Copy).then_inc(h_high, 1)

            def copy_y(down_done, u):
                act.wait_ge(used, down_done)
                act.activation(y[:, u, :], ps[:, DOWN[0]:DOWN[1] + 1, :].rearrange("p b n -> p (b n)"), ACT.Copy).then_inc(y_ready, 1)

            def block_steps(e, u, count, stored, last=False):
                down_high(down_piece(e - 1), 1 - u, AT[u] + GU_PIECES, count)
                if not last:
                    gate_high(e + 1, 1 - u, AT[1 - u], count + 1)
                act.wait_ge(hb_ready, e)
                silu(gu_piece(e) + GATE_PIECES)
                if not last:
                    x_to_high(e + 1, 1 - u)
                    up_high(e + 1, 1 - u, AT[1 - u], count + 1)
                if stored is not None:
                    act.wait_ge(y_stored[1 - u], 16 * stored)
                copy_y(down_piece(e - 1) + ET, 1 - u)
                h_to_high(e)

            act.wait_ge(loaded[0][0], 16)
            for q in range(GATE_PIECES):
                split_high(q, q, raw(0, q))
            x_to_high(0, 0)
            act.wait_ge(loaded[1][0], 16)
            for q in range(GATE_PIECES, GU_PIECES):
                split_high(q, q, raw(0, q))
            gate_high(1, 1, 0, 1)
            silu(GATE_PIECES)
            x_to_high(1, 1)
            up_high(1, 1, 0, 1)
            h_to_high(0)
            block_steps(1, 1, 1, None)
            block_steps(2, 0, 1, None)
            with act.Fori(1, NE // 2 - 1) as i:
                block_steps(2 * i + 1, 1, i + 1, i)
                block_steps(2 * i + 2, 0, i + 1, i)
            block_steps(NE - 1, 1, NE // 2, NE // 2 - 1, last=True)
            down_high(NPIECE * NE - ET, 1, AT[0], NE // 2)
            act.wait_ge(y_stored[1], 16 * (NE // 2 - 1))
            copy_y(NPIECE * NE, 1)
            n_over = over_loop(act)
            with act.If(n_over > 0):
                for u in range(2):
                    act.wait_ge(y_stored[u], 16 * NE // 2)
                with act.Fori(0, n_over) as j:
                    n = NPIECE * (NE + j)
                    act.wait_ge(o_loaded, j * 48 + 48)
                    x_to_high(j + NE, 0)
                    for q in range(NPIECE):
                        if q == GU_PIECES:
                            act.wait_ge(hb_ready, j + NE)
                            silu(n + GATE_PIECES)
                        if q >= AHEAD:
                            act.wait_ge(used, n + q - AHEAD + 1)
                        act.activation(hw[:, q % AHEAD, :], raw(0, q), ACT.Copy).then_inc(high, 1)
                    h_to_high(j + NE)
                    copy_y(n + NPIECE, 0)
            for i in range(T):
                act.wait_ge(combined, 2 * i + 2)
                if i >= 1:
                    act.wait_ge(f_sq, i)
                act.activation(sq[:, :], h[:, i, :], ACT.Square, accum_out=ssum[:, i:i + 1]).then_inc(f_sq, 1)
                if after:
                    act.wait_ge(f_mean, i + 1)
                    act.activation(rms[:, i:i + 1], ssum[:, i:i + 1], ACT.Sqrt).then_inc(f_root, 1)

        @block.tensor
        def _(pe):
            pe.wait_ge(small_loaded, 64)
            pe.wait_ge(consts, 8)

            def turn_rows(src, pair=0):
                for k in range(KT):
                    last = pe.transpose(turn_ps(pair)[:, k, :], src[:, k * P:(k + 1) * P], ident[:, :])
                return last

            for i in range(T):
                pe.wait_ge(hr_ready, i + 1)
                if i >= 2:
                    pe.wait_ge(hnT_ready, i - 1)
                turn_rows(hr[:, i % 2, :], i % 2).then_inc(turned, 1)
                if i >= 1:
                    pe.wait_ge(hnT_ready, i)
                    for k in range(KT):
                        last = pe.matmul(ps[:, ROUTE, (i - 1) * NR:i * NR], hnT[:, (i - 1) % 2, k, :], wr[:, k, :],
                                         start=(k == 0), stop=(k == KT - 1))
                    last.then_inc(routed, 1)
            pe.wait_ge(hnT_ready, T)
            for k in range(KT):
                last = pe.matmul(ps[:, ROUTE, (T - 1) * NR:T * NR], hnT[:, (T - 1) % 2, k, :], wr[:, k, :],
                                 start=(k == 0), stop=(k == KT - 1))
            last.then_inc(routed, 1)
            pe.wait_ge(ohb_ready, 1)
            for i in range(T):
                for j in range(i):
                    pe.matmul(ps[:, RANK, i * NE:(i + 1) * NE], ones_b[:, :], ohb[:, j, :], start=(j == 0), stop=False)
                pe.matmul(ps[:, RANK, i * NE:(i + 1) * NE], tri_b[:, :], ohb[:, i, :], start=(i == 0), stop=True)
            for j in range(T):
                last = pe.matmul(ps[:, RANK, T * NE:(T + 1) * NE], ones_b[:, :], ohb[:, j, :], start=(j == 0), stop=(j == T - 1))
            last.then_inc(ranked, 1)
            pe.wait_ge(ab_ready, 1)
            for n in range(2 * T):
                last = pe.matmul(ps[:, ROUTE, 0:NBLK], Am[:, n, :], Bm[:, n, :], start=(n == 0), stop=(n == 2 * T - 1))
            last.then_inc(listed, 1)

            def turn_x(e, u, arrived, count):
                pe.wait_ge(arrived, count)
                pe.wait_ge(x_low, e)
                turn_rows(xg[:, u, :]).then_inc(x_turned, 1)

            def gate_up(e, u, first, at):
                pe.wait_ge(x_low, e + 1)
                for q in range(GU_PIECES):
                    pe.wait_ge(low, first + q + 1)
                    for s in range(2):
                        k = 2 * (q % GATE_PIECES) + s
                        cols = slice(s * DE, (s + 1) * DE)
                        last = split_product(pe, ps[:, GATE if q < GATE_PIECES else UP, :], xhl[:, u, 0, k, :], xhl[:, u, 1, k, :],
                                       hw[:, (at + q) % AHEAD, cols], lowp(u, q)[:, cols], k == 0, k == KT - 1)
                    last.then_inc(used, 1)

            def turn_h(e):
                pe.wait_ge(hb_ready, e + 1)
                for k in range(ET):
                    last = pe.transpose(ps[:, HT, k * P:(k + 1) * P], hb[:, k * P:(k + 1) * P], ident[:, :])
                last.then_inc(h_turned, 1)

            def down(e, u, first, at):
                pe.wait_ge(h_low, e + 1)
                for k in range(ET):
                    pe.wait_ge(low, first + k + 1)
                    for b in range(2):
                        cols = slice(b * HALF, (b + 1) * HALF)
                        last = split_product(pe, ps[:, DOWN[b], :], hhl[:, 0, k, :], hhl[:, 1, k, :],
                                       hw[:, (at + k) % AHEAD, cols], lowp(u, GU_PIECES + k)[:, cols], k == 0, k == ET - 1)
                    last.then_inc(used, 1)

            def block_steps(e, u, count, last=False):
                gate_up(e, u, gu_piece(e), AT[u])
                if not last:
                    turn_x(e + 1, 1 - u, xg_loaded[1 - u], 16 * count)
                pe.wait_ge(y_ready, e - 1)
                down(e - 1, 1 - u, down_piece(e - 1), AT[u] + GU_PIECES)
                turn_h(e)

            pe.wait_ge(xg_loaded[0], 16)
            pe.wait_ge(lists_ready, 1)
            turn_rows(xg[:, 0, :]).then_inc(x_turned, 1)
            gate_up(0, 0, 0, 0)
            turn_x(1, 1, xg_loaded[1], 16)
            turn_h(0)
            gate_up(1, 1, gu_piece(1), AT[1])
            turn_x(2, 0, xg_loaded[0], 32)
            down(0, 0, down_piece(0), AT[1] + GU_PIECES)
            turn_h(1)
            with pe.Fori(1, NE // 2 - 1) as i:
                block_steps(2 * i, 0, i + 1)
                block_steps(2 * i + 1, 1, i + 2)
            block_steps(NE - 2, 0, NE // 2)
            block_steps(NE - 1, 1, None, last=True)
            pe.wait_ge(y_ready, NE - 1)
            down(NE - 1, 1, NPIECE * NE - ET, AT[0])
            n_over = over_loop(pe)
            with pe.If(n_over > 0):
                with pe.Fori(0, n_over) as j:
                    e = j + NE
                    turn_x(e, 0, o_gathered, j * 16 + 16)
                    gate_up(e, 0, NPIECE * e, 0)
                    turn_h(e)
                    pe.wait_ge(y_ready, e)
                    down(e, 0, NPIECE * e + GU_PIECES, GU_PIECES)

        @block.vector
        def _(dve):
            count = [0]

            def chain(ins):
                count[0] += 1
                ins.then_inc(step, 1)
                dve.wait_ge(step, count[0])

            def tt(out, a, b, op):
                chain(dve.tensor_tensor(out, a, b, op))

            def ts(out, a, s1, s2, op0, op1=ALU.bypass):
                chain(dve.tensor_scalar(out, a, s1, s2, op0, op1))

            dve.wait_ge(small_loaded, 64)
            def evacuate(i):
                dve.wait_ge(turned, i + 1)
                if i >= 2:
                    dve.wait_ge(routed, i - 1)
                dve.tensor_copy(hnT[:, i % 2, :, :], turn_ps(i % 2)).then_inc(hnT_ready, 1)

            dve.tensor_scalar(ssum[:, :], ssum[:, :], 1.0 / D, EPS, ALU.mult, ALU.add).then_inc(meaned, 1)
            dve.wait_ge(rooted, 1)
            chain(dve.reciprocal(rinv[:, :], rms[:, :]))
            for i in range(T):
                if i >= 2:
                    dve.wait_ge(hr_stored[i % 2], 16 * (i // 2))
                    dve.wait_ge(turned, i - 1)
                if i == 0:
                    dve.wait_ge(gains_loaded, 16)
                dve.scalar_tensor_tensor(hr[:, i % 2, :], h[:, i, :], rinv[:, i:i + 1], gains[:, :], ALU.mult, ALU.mult).then_inc(hr_ready, 1)
                if i >= 1:
                    evacuate(i - 1)
            evacuate(T - 1)

            dve.wait_ge(routed, T)
            dve.wait_ge(consts, 8)
            psR = ps[:, ROUTE, 0:T * NR].rearrange("p (t n) -> p t n", t=T)
            tt(lg[:, :, :], psR, rbias[:, :].unsqueeze(1).to_broadcast([P, T, NR]), ALU.add)
            gl, el = lg[:, :, 0:NG], lg[:, :, NG:NR]
            gmax, gp, gsum, ggate, diff, ed, m1, m2, p1, den = (small[:, n, :] for n in (0, 1, 2, 3, 4, 5, 6, 7, 8, 9))

            def bc(v, n):
                return v.unsqueeze(2).to_broadcast([P, T, n])

            def first_best(out, values, best, prio, pbest, tmp, n):
                chain(dve.tensor_reduce(best, values, AX.X, ALU.max))
                tt(tmp, values, bc(best, n), ALU.is_equal)
                tt(tmp, tmp, prio.unsqueeze(1).to_broadcast([P, T, n]), ALU.mult)
                chain(dve.tensor_reduce(pbest, tmp, AX.X, ALU.max))
                tt(out, tmp, bc(pbest, n), ALU.is_equal)

            first_best(goh[:, :, :], gl, gmax, pri[:, 0:NG], gp, ga[:, :, :], NG)
            dve.tensor_tensor(ga[:, :, :], gl, bc(gmax, NG), ALU.subtract).then_inc(ebias, 1)
            ts(slotm[:, :, 0:NG], goh[:, :, :], NEG, -NEG, ALU.mult, ALU.add)
            for t in range(T):
                last = dve.tensor_tensor(em[:, t, :].rearrange("p (g n) -> p g n", g=NG),
                                         lg[:, t, NG:NR].rearrange("p (g n) -> p g n", g=NG),
                                         slotm[:, t, 0:NG].unsqueeze(2).to_broadcast([P, NG, NPG]), ALU.add)
            chain(last)
            first_best(oh[:, 0, :, :], em[:, :, :], m1, pri[:, :], p1, ea[:, :, :], NE)
            chain(dve.scalar_tensor_tensor(em[:, :, :], oh[:, 0, :, :], -2 * NEG, em[:, :, :], ALU.mult, ALU.add))
            first_best(oh[:, 1, :, :], em[:, :, :], m2, pri[:, :], p1, ea[:, :, :], NE)
            dve.tensor_tensor(diff, m2, m1, ALU.subtract).then_inc(ebias, 1)
            dve.tensor_tensor(ohb[:, :, :], oh[:, 0, :, :], oh[:, 1, :, :], ALU.add).then_inc(ohb_ready, 1)
            dve.wait_ge(expd, 2)
            chain(dve.tensor_reduce(gsum, ga[:, :, :], AX.X, ALU.add))
            chain(dve.reciprocal(ggate, gsum))
            ts(den, ed, 1.0, None, ALU.add)
            chain(dve.reciprocal(p1, den))
            tt(wts[:, 0, :], p1, ggate, ALU.mult)
            tt(wts[:, 1, :], wts[:, 0, :], ed, ALU.mult)
            dve.wait_ge(ranked, 1)
            psK = ps[:, RANK, 0:T * NE].rearrange("p (t n) -> p t n", t=T)
            ts(novi[:, :], ps[:, RANK, T * NE:(T + 1) * NE], float(P - 1), None, ALU.add)
            ts(novi[:, :], novi[:, :], 7, None, ALU.arith_shift_right)
            chain(dve.tensor_copy(novf[:, :], novi[:, :]))
            ts(novf[:, :], novf[:, :], -1.0, 0.0, ALU.add, ALU.max)
            chain(dve.tensor_tensor_scan(obend[:, :], novf[:, :], zeros[:, :], 0.0, ALU.add, ALU.add))
            tt(dlt[:, :], obend[:, :], novf[:, :], ALU.subtract)
            ts(dlt[:, :], dlt[:, :], float(P), float((NE - 1) * P), ALU.mult, ALU.add)
            tt(dlt[:, :], dlt[:, :], cap1[:, :], ALU.subtract)
            ts(slotm[:, :, :], psK, float(P), None, ALU.is_ge)
            tt(slotm[:, :, :], slotm[:, :, :], dlt[:, :].unsqueeze(1).to_broadcast([P, T, NE]), ALU.mult)
            tt(slotm[:, :, :], slotm[:, :, :], psK, ALU.add)
            tt(slotm[:, :, :], slotm[:, :, :], cap1[:, :].unsqueeze(1).to_broadcast([P, T, NE]), ALU.add)
            for a in range(2):
                tt(ea, slotm, oh[:, a, :, :], ALU.mult)
                chain(dve.tensor_reduce(slot[:, a, :], ea[:, :, :], AX.X, ALU.add))
            chain(dve.tensor_copy(sloti[:, :, :], slot[:, :, :]))
            chain(dve.tensor_copy(slotu[:, :], slot[:, :, :].rearrange("p a t -> p (a t)")))
            ts(blki[:, :, :], sloti[:, :, :], 7, None, ALU.arith_shift_right)
            ts(loi[:, :, :], sloti[:, :, :], P - 1, None, ALU.bitwise_and)
            chain(dve.tensor_copy(blk[:, :, :], blki[:, :, :]))
            chain(dve.tensor_copy(lo[:, :, :], loi[:, :, :]))
            for u in range(2):
                dve.wait_ge(hr_stored[u], 16 * T // 2)
            for a in range(2):
                for t in range(T):
                    dve.tensor_scalar(Am[:, a * T + t, :], iota[:, :], lo[:, a, t:t + 1], None, ALU.is_equal)
                    last = dve.tensor_scalar(Bm[:, a * T + t, :], iota[:, 0:NBLK], blk[:, a, t:t + 1], tokid[:, t:t + 1],
                                             ALU.is_equal, ALU.mult)
            last.then_inc(ab_ready, 1)
            tt(eidc[:, :, :], obend[:, :].unsqueeze(1).to_broadcast([P, NOVER, NE]),
               iota[:, 0:NOVER].unsqueeze(2).to_broadcast([P, NOVER, NE]), ALU.is_le)
            chain(dve.tensor_reduce(eid[:, :], eidc[:, :, :], AX.X, ALU.add))
            chain(dve.tensor_copy(eidi[:, 0:NOVER], eid[:, :]))
            chain(dve.tensor_copy(eidi[:, NOVER:NOVER + 1], obend[:, NE - 1:NE]))
            dve.wait_ge(listed, 1)
            dve.tensor_copy(toku[:, :], ps[:, ROUTE, 0:NBLK]).then_inc(lists_ready, 1)

            def split_low(n, at, u, q):
                dve.wait_ge(high, n + 1)
                dve.tensor_tensor(lowp(u, q), raw(u, q), hw[:, at % AHEAD, :].bitcast(F32), ALU.subtract).then_inc(low, 1)

            def gate_low(e, u, at):
                for q in range(GATE_PIECES):
                    split_low(gu_piece(e) + q, at + q, u, q)

            def up_low(e, u, at):
                for q in range(GATE_PIECES, GU_PIECES):
                    split_low(gu_piece(e) + q, at + q, u, q)

            def down_low(first, u, at):
                for q in range(ET):
                    split_low(first + q, at + q, u, GU_PIECES + q)

            def x_to_low(e, u):
                dve.wait_ge(x_high, e + 1)
                dve.tensor_tensor(xhl[:, u, 1, :, :], turn_ps(), xhl[:, u, 0, :, :].bitcast(F32), ALU.subtract).then_inc(x_low, 1)

            def product(e, up_done):
                dve.wait_ge(used, up_done)
                dve.wait_ge(silu_done, e + 1)
                dve.tensor_tensor(hb, sg, ps[:, UP, :], ALU.mult).then_inc(hb_ready, 1)

            def h_to_low(e):
                dve.wait_ge(h_high, e + 1)
                dve.tensor_tensor(hhl[:, 1, :, :], ps[:, HT, :].rearrange("p (k c) -> p k c", c=P), hhl[:, 0, :, :].bitcast(F32),
                                  ALU.subtract).then_inc(h_low, 1)

            def block_steps(e, u, last=False):
                down_low(down_piece(e - 1), 1 - u, AT[u] + GU_PIECES)
                if not last:
                    gate_low(e + 1, 1 - u, AT[1 - u])
                product(e, gu_piece(e) + GU_PIECES)
                if not last:
                    x_to_low(e + 1, 1 - u)
                    up_low(e + 1, 1 - u, AT[1 - u])
                h_to_low(e)

            for q in range(GATE_PIECES):
                split_low(q, q, 0, q)
            x_to_low(0, 0)
            for q in range(GATE_PIECES, GU_PIECES):
                split_low(q, q, 0, q)
            gate_low(1, 1, 0)
            product(0, GU_PIECES)
            x_to_low(1, 1)
            up_low(1, 1, 0)
            h_to_low(0)
            with dve.Fori(0, NE // 2 - 1) as i:
                block_steps(2 * i + 1, 1)
                block_steps(2 * i + 2, 0)
            block_steps(NE - 1, 1, last=True)
            down_low(NPIECE * NE - ET, 1, AT[0])
            n_over = over_loop(dve)
            with dve.If(n_over > 0):
                for u in range(2):
                    dve.wait_ge(y_stored[u], 16 * NE // 2)
                with dve.Fori(0, n_over) as j:
                    n = NPIECE * (NE + j)
                    dve.wait_ge(o_loaded, j * 48 + 48)
                    x_to_low(j + NE, 0)
                    for q in range(NPIECE):
                        if q == GU_PIECES:
                            product(j + NE, n + GU_PIECES)
                        dve.wait_ge(high, n + q + 1)
                        dve.tensor_tensor(lowp(0, q), raw(0, q), hw[:, q % AHEAD, :].bitcast(F32), ALU.subtract).then_inc(low, 1)
                    h_to_low(j + NE)

            for i in range(T):
                dve.wait_ge(r_loaded[i % ROWBUFS], 32 * (i // ROWBUFS + 1))
                dve.scalar_tensor_tensor(h[:, i, :], rows[:, i % ROWBUFS, 0, :], wts[:, 0, i:i + 1], h[:, i, :],
                                         ALU.mult, ALU.add).then_inc(combined, 1)
                dve.wait_ge(combined, 2 * i + 1)
                dve.scalar_tensor_tensor(h[:, i, :], rows[:, i % ROWBUFS, 1, :], wts[:, 1, i:i + 1], h[:, i, :],
                                         ALU.mult, ALU.add).then_inc(combined, 1)
                if after:
                    dve.wait_ge(f_sq, i + 1)
                    dve.tensor_scalar(ssum[:, i:i + 1], ssum[:, i:i + 1], 1.0 / D, EPS, ALU.mult, ALU.add).then_inc(f_mean, 1)
                    dve.wait_ge(f_root, i + 1)
                    chain(dve.reciprocal(rinv[:, i:i + 1], rms[:, i:i + 1]))
                    if i == 0:
                        dve.wait_ge(final_loaded, 16)
                    if i >= 2:
                        dve.wait_ge(f_stored[i % 2], 16 * (i // 2))
                    dve.scalar_tensor_tensor(hnT[:, i % 2, :, :].rearrange("p k c -> p (k c)"), h[:, i, :], rinv[:, i:i + 1],
                                             gains[:, :], ALU.mult, ALU.mult).then_inc(f_out, 1)


def setup(nc, g, ctx, arrays):
    g.of_block = []
    g.dram = arrays
    g.h = ctx.enter_context(nc.sbuf_tensor("h", [P, T, D], F32))
    g.ring = ctx.enter_context(nc.sbuf_tensor("ring", [P, 2 * SLOT], F32))
    g.ring_at = nc.sbuf_base - 4 * 2 * SLOT
    g.ident = ctx.enter_context(nc.sbuf_tensor("ident", [P, P], F32))
    g.mean_w = ctx.enter_context(nc.sbuf_tensor("mean_w", [P, P], F32))
    g.vecs = ctx.enter_context(nc.sbuf_tensor("vecs", [P, V_ROWS], F32))
    g.ssum = ctx.enter_context(nc.sbuf_tensor("ssum", [P, T], F32))
    g.ps = ctx.enter_context(nc.psum_tensor("ps", [P, 8, HALF], F32))
    g.y_dram = nc.dram_tensor("y_dram", [NBLK * P, D], F32, kind="Internal").ap()


def hybrid_kernel(nc, arrays):
    with ExitStack() as ctx:
        g = Shared()
        setup(nc, g, ctx, arrays)
        conv_block(nc, g)
        g.end_block(nc)
        moe_block(nc, g, 0, False)
        g.end_block(nc)
        attention_block(nc, g)
        g.end_block(nc)
        moe_block(nc, g, 1, True)


def rope_tables():
    import numpy as np
    inv = np.float32(ROPE_THETA) ** (-np.arange(0, ROT, 2, dtype=np.float32) / np.float32(ROT))
    ang = np.arange(S, dtype=np.float32)[:, None] * inv.astype(np.float32)[None, :]
    return np.stack([np.cos(ang), np.sin(ang)]).astype(np.float32)


_INS = ['x', 'mix_norm_g', 'ffn_norm_g', 'final_norm_g', 'conv_w_in', 'conv_b_in', 'conv_w_dw', 'conv_b_dw', 'conv_ln_g',
        'conv_ln_b', 'conv_w_out', 'conv_b_out', 'attn_w_in', 'idx_k_ln_g', 'idx_k_ln_b', 'attn_w_out', 'moe_w_group',
        'moe_b_group', 'moe_w_router', 'moe_b_router', 'moe_w_gate', 'moe_w_up', 'moe_w_down']


def kernel(**inputs):
    import numpy as np
    import concourse.bacc as bacc
    from concourse.bass_utils import run_bass_kernel_spmd

    nc = bacc.Bacc("TRN2", target_bir_lowering=False, num_devices=1)
    given = {name: np.ascontiguousarray(inputs[name]) for name in _INS}
    given["rope"] = rope_tables()
    arrays = {}
    for name, a in given.items():
        arrays[name] = nc.dram_tensor(f"in_{name}_dram", a.shape, mybir.dt.from_np(a.dtype), kind="ExternalInput").ap()
    arrays["out"] = nc.dram_tensor("out_dram", (1, S, D), F32, kind="ExternalOutput").ap()
    hybrid_kernel(nc, arrays)
    r = run_bass_kernel_spmd(nc, [{f"in_{name}_dram": a for name, a in given.items()}], core_ids=[0])
    return r.results[0]["out_dram"]
```
